# Optimizing a Trainium2 kernel written in Bass

```python
import jax, jax.numpy as jnp
from jax import lax
import numpy as np

D_MODEL = 1024
BATCH = 1
SEQ = 256
DEPTH = 1
DEC_BATCH = 8
DEC_SEQ = 1
PAST_LEN = 2048
PAGE_SIZE = 128

D_MIX = D_MODEL
DA = D_MIX // 2
H_A = 8
BH = DA // H_A
DB = D_MIX - DA
H_B = 4
DV = DB // H_B
DK = DV // 2
GATE_RANK = 16
GATE_TAU = 16.0
GLA_CHUNK = 64
CONV_W = 4
C_RG = 8.0
IN_COLS = 2 * DA + 2 * H_B * DK + 2 * DB + GATE_RANK
N_EXPERTS = 32
TOP_K = 4
D_FF = D_MODEL
SWIGLU_ALPHA = 1.702
SWIGLU_LIMIT = 7.0
MOE_BLOCK = 128
N_META = 16
EPS = 1e-6

kernel_name = 'hymba_rglru_gla_moe_step'

def _rmsnorm(x, g):
    x32 = x.astype(jnp.float32)
    y = x32 * lax.rsqrt(jnp.mean(x32 * x32, axis=-1, keepdims=True) + EPS)
    return (y * g.astype(jnp.float32)).astype(x.dtype)

def _lru_combine(left, right):
    a_l, b_l = left
    a_r, b_r = right
    return a_l * a_r, a_r * b_l + b_r

def _rglru(xc, r_logit, i_logit, lam, h0):
    r = jax.nn.sigmoid(r_logit.astype(jnp.float32))
    i = jax.nn.sigmoid(i_logit.astype(jnp.float32))
    log_a = -C_RG * r * jax.nn.softplus(-lam.astype(jnp.float32))
    a = jnp.exp(log_a)
    b = jnp.sqrt(-jnp.expm1(2.0 * log_a)) * i * xc.astype(jnp.float32)
    b = b.at[:, 0].add(a[:, 0] * h0.astype(jnp.float32))
    _, hs = lax.associative_scan(_lru_combine, (a, b), axis=1)
    return hs, hs[:, -1]

def _gla_chunk(S, q, k, v, la):
    L = q.shape[1]
    b = jnp.cumsum(la, axis=1)
    o_inter = jnp.einsum('blhk,bhkv->blhv', q * jnp.exp(b), S)
    causal = jnp.tril(jnp.ones((L, L), dtype=bool))[None, :, :, None, None]
    decay = jnp.exp(jnp.where(causal, b[:, :, None] - b[:, None, :], -jnp.inf))
    scores = jnp.einsum('bthk,btshk->bhts', q, decay * k[:, None])
    o_intra = jnp.einsum('bhts,bshv->bthv', scores, v)
    b_last = b[:, -1]
    S_new = jnp.exp(b_last)[..., None] * S + jnp.einsum(
        'bshk,bshv->bhkv', k * jnp.exp(b_last[:, None] - b), v)
    return S_new, o_inter + o_intra

def _gla(q, k, v, la, S0, lead):
    T = q.shape[1]
    S, o_lead = _gla_chunk(S0, q[:, :lead], k[:, :lead], v[:, :lead], la[:, :lead])
    outs = [o_lead]
    n_full = (T - lead) // GLA_CHUNK
    end = lead + n_full * GLA_CHUNK
    if n_full > 0:
        def to_chunks(t):
            t = t[:, lead:end]
            return jnp.moveaxis(t.reshape(t.shape[0], n_full, GLA_CHUNK, *t.shape[2:]), 1, 0)
        S, o_main = lax.scan(lambda s, xs: _gla_chunk(s, *xs), S,
                             (to_chunks(q), to_chunks(k), to_chunks(v), to_chunks(la)))
        o_main = jnp.moveaxis(o_main, 0, 1)
        outs.append(o_main.reshape(o_main.shape[0], n_full * GLA_CHUNK, *o_main.shape[3:]))
    if end < T:
        S, o_tail = _gla_chunk(S, q[:, end:], k[:, end:], v[:, end:], la[:, end:])
        outs.append(o_tail)
    return jnp.concatenate(outs, axis=1), S

def _moe(u, w_router, b_router, w_gu, b_gu, w_down, b_down):
    n_tok, d = u.shape
    n_asg = n_tok * TOP_K
    logits = u.astype(jnp.float32) @ w_router.astype(jnp.float32) + b_router.astype(jnp.float32)
    top_val, top_idx = lax.top_k(logits, TOP_K)
    gates = jax.nn.softmax(top_val, axis=-1)
    flat_e = top_idx.reshape(-1)
    flat_tok = jnp.arange(n_asg, dtype=jnp.int32) // TOP_K
    flat_w = gates.reshape(-1)
    order = jnp.argsort(flat_e)
    e_sorted = flat_e[order]
    counts = jnp.bincount(flat_e, length=N_EXPERTS)
    padded = (counts + MOE_BLOCK - 1) // MOE_BLOCK * MOE_BLOCK
    pad_end = jnp.cumsum(padded)
    pad_start = pad_end - padded
    grp_start = jnp.cumsum(counts) - counts
    dest = pad_start[e_sorted] + jnp.arange(n_asg, dtype=jnp.int32) - grp_start[e_sorted]
    n_blk = -(-n_asg // MOE_BLOCK) + N_EXPERTS
    n_rows = n_blk * MOE_BLOCK
    row_tok = jnp.full((n_rows,), n_tok, jnp.int32).at[dest].set(flat_tok[order])
    row_w = jnp.zeros((n_rows,), jnp.float32).at[dest].set(flat_w[order])
    blk_e = jnp.minimum(jnp.searchsorted(pad_end, jnp.arange(n_blk) * MOE_BLOCK, side='right'),
                        N_EXPERTS - 1)
    u_pad = jnp.concatenate([u, jnp.zeros((1, d), u.dtype)], axis=0)

    def expert_block(args):
        tok, e = args
        xb = u_pad[tok]
        gu = xb @ w_gu[e] + b_gu[e]
        gate = jnp.minimum(gu[:, :D_FF], SWIGLU_LIMIT)
        lin = jnp.clip(gu[:, D_FF:], -SWIGLU_LIMIT, SWIGLU_LIMIT)
        act = (lin + 1.0) * gate * jax.nn.sigmoid(SWIGLU_ALPHA * gate)
        return act @ w_down[e] + b_down[e]

    y_rows = lax.map(expert_block, (row_tok.reshape(n_blk, MOE_BLOCK), blk_e))
    y = jnp.zeros((n_tok + 1, d), jnp.float32).at[row_tok].add(
        y_rows.reshape(n_rows, d).astype(jnp.float32) * row_w[:, None])
    return y[:n_tok].astype(u.dtype)

def _layer(h, conv_buf, h0, S0, lead, g_mix, w_in, conv_w, conv_b, w_rg_a, b_rg_a, w_rg_x,
           b_rg_x, lam, gn_a, w_gate_up, b_gate, gn_b, w_out, g_ffn, w_router, b_router,
           w_gu, b_gu, w_down, b_down):
    B, T, D = h.shape
    dt = h.dtype
    u = _rmsnorm(h, g_mix)
    proj = u @ w_in
    split_idx = np.cumsum([DA, DA, H_B * DK, H_B * DK, DB, DB]).tolist()
    xa, ya, q, k, v, g, lr = jnp.split(proj, split_idx, axis=-1)
    xa_ext = jnp.concatenate([conv_buf.astype(xa.dtype), xa], axis=1)
    xc = conv_b + sum(xa_ext[:, j:j + T] * conv_w[j] for j in range(CONV_W))
    conv_new = xa_ext[:, T:]
    xh = xc.reshape(B, T, H_A, BH)
    r_logit = jnp.einsum('bthi,hij->bthj', xh, w_rg_a).reshape(B, T, DA) + b_rg_a
    i_logit = jnp.einsum('bthi,hij->bthj', xh, w_rg_x).reshape(B, T, DA) + b_rg_x
    hs, h_last = _rglru(xc, r_logit, i_logit, lam, h0)
    out_a = _rmsnorm(hs.astype(dt) * jax.nn.gelu(ya), gn_a)
    q32 = q.reshape(B, T, H_B, DK).astype(jnp.float32) * DK ** -0.5
    k32 = k.reshape(B, T, H_B, DK).astype(jnp.float32)
    v32 = v.reshape(B, T, H_B, DV).astype(jnp.float32)
    la = jax.nn.log_sigmoid((lr @ w_gate_up + b_gate).astype(jnp.float32)) / GATE_TAU
    o, S_new = _gla(q32, k32, v32, la.reshape(B, T, H_B, DK), S0.astype(jnp.float32), lead)
    out_b = _rmsnorm(o.astype(dt), gn_b).reshape(B, T, DB) * jax.nn.silu(g)
    h = h + jnp.concatenate([out_a, out_b], axis=-1) @ w_out
    u2 = _rmsnorm(h, g_ffn)
    h = h + _moe(u2.reshape(B * T, D), w_router, b_router, w_gu, b_gu, w_down,
                 b_down).reshape(B, T, D)
    return h, conv_new, h_last, S_new

def setup_inputs(seed: int = 0) -> dict:
    key = jax.random.key(seed)
    ks = iter(jax.random.split(key, 40))
    nrm = lambda shape, scale: scale * jax.random.normal(next(ks), shape, jnp.float32)
    a_base = jax.random.uniform(next(ks), (DEPTH, DA), jnp.float32, 0.9, 0.999) ** (1.0 / C_RG)
    lam = jnp.log(a_base) - jnp.log1p(-a_base)
    return {
        'x_prompt': nrm((BATCH, SEQ, D_MODEL), 1.0),
        'x_sample': nrm((DEC_BATCH, DEC_SEQ, D_MODEL), 1.0),
        'state_conv': nrm((DEPTH, DEC_BATCH, CONV_W - 1, DA), 1.0),
        'state_lru': nrm((DEPTH, DEC_BATCH, DA), 0.5),
        'state_gla': nrm((DEPTH, DEC_BATCH, H_B, DK, DV), 0.5),
        'meta': nrm((N_META, D_MODEL), 1.0),
        'g_mix': 1.0 + nrm((DEPTH, D_MODEL), 0.02),
        'w_in': nrm((DEPTH, D_MODEL, IN_COLS), D_MODEL ** -0.5),
        'conv_w': nrm((DEPTH, CONV_W, DA), CONV_W ** -0.5),
        'conv_b': nrm((DEPTH, DA), 0.02),
        'w_rg_a': nrm((DEPTH, H_A, BH, BH), BH ** -0.5),
        'b_rg_a': nrm((DEPTH, DA), 0.02),
        'w_rg_x': nrm((DEPTH, H_A, BH, BH), BH ** -0.5),
        'b_rg_x': nrm((DEPTH, DA), 0.02),
        'lam': lam,
        'gn_a': 1.0 + nrm((DEPTH, DA), 0.02),
        'w_gate_up': nrm((DEPTH, GATE_RANK, H_B * DK), GATE_RANK ** -0.5),
        'b_gate': nrm((DEPTH, H_B * DK), 0.1),
        'gn_b': 1.0 + nrm((DEPTH, DV), 0.02),
        'w_out': nrm((DEPTH, D_MIX, D_MODEL), D_MIX ** -0.5),
        'g_ffn': 1.0 + nrm((DEPTH, D_MODEL), 0.02),
        'w_router': nrm((DEPTH, D_MODEL, N_EXPERTS), D_MODEL ** -0.5),
        'b_router': nrm((DEPTH, N_EXPERTS), 0.01),
        'w_gu': nrm((DEPTH, N_EXPERTS, D_MODEL, 2 * D_FF), D_MODEL ** -0.5),
        'b_gu': nrm((DEPTH, N_EXPERTS, 2 * D_FF), 0.02),
        'w_down': nrm((DEPTH, N_EXPERTS, D_FF, D_MODEL), D_FF ** -0.5),
        'b_down': nrm((DEPTH, N_EXPERTS, D_MODEL), 0.02),
        'g_final': 1.0 + nrm((D_MODEL,), 0.02),
    }

def reference(x_prompt, x_sample, state_conv, state_lru, state_gla, meta, g_mix, w_in, conv_w,
              conv_b, w_rg_a, b_rg_a, w_rg_x, b_rg_x, lam, gn_a, w_gate_up, b_gate, gn_b,
              w_out, g_ffn, w_router, b_router, w_gu, b_gu, w_down, b_down, g_final):
    B = x_prompt.shape[0]
    dt = x_prompt.dtype
    hp = jnp.concatenate([jnp.broadcast_to(meta.astype(dt)[None], (B, N_META, D_MODEL)),
                          x_prompt], axis=1)
    hs = x_sample
    conv_p_l, lru_p_l, gla_p_l, conv_s_l, lru_s_l, gla_s_l = [], [], [], [], [], []
    for l in range(DEPTH):
        wl = (g_mix[l], w_in[l], conv_w[l], conv_b[l], w_rg_a[l], b_rg_a[l], w_rg_x[l],
              b_rg_x[l], lam[l], gn_a[l], w_gate_up[l], b_gate[l], gn_b[l], w_out[l], g_ffn[l],
              w_router[l], b_router[l], w_gu[l], b_gu[l], w_down[l], b_down[l])
        hp, c_p, r_p, s_p = _layer(hp, jnp.zeros((B, CONV_W - 1, DA), dt),
                                   jnp.zeros((B, DA), jnp.float32),
                                   jnp.zeros((B, H_B, DK, DV), jnp.float32), N_META, *wl)
        hs, c_s, r_s, s_s = _layer(hs, state_conv[l], state_lru[l], state_gla[l],
                                   hs.shape[1], *wl)
        conv_p_l.append(c_p); lru_p_l.append(r_p); gla_p_l.append(s_p)
        conv_s_l.append(c_s); lru_s_l.append(r_s); gla_s_l.append(s_s)
    y_prompt = _rmsnorm(hp[:, N_META:], g_final)
    y_sample = _rmsnorm(hs, g_final)
    return (y_prompt, y_sample, jnp.stack(conv_p_l), jnp.stack(lru_p_l), jnp.stack(gla_p_l),
            jnp.stack(conv_s_l), jnp.stack(lru_s_l), jnp.stack(gla_s_l))


_drawn_inputs = setup_inputs


def setup_inputs(seed=0):
    import zlib

    import numpy as np

    out = dict(_drawn_inputs(seed))
    spreads = {}
    factors = {'b_rg_a': 5.676, 'b_rg_x': 4.087, 'b_gu': 6.325, 'b_down': 7.29, 'g_final': 3.073}
    for name, (base, spread) in spreads.items():
        noise = np.random.default_rng([zlib.crc32(name.encode()), seed]).standard_normal(out[name].shape)
        drawn = base * np.exp(spread * noise) if base else spread * noise
        out[name] = __import__('jax').numpy.asarray(drawn.astype(out[name].dtype))
    for name, factor in factors.items():
        out[name] = (out[name] * factor).astype(out[name].dtype)
    return out
```

```python
import concourse.bass as bass
from concourse import mybir
from contextlib import ExitStack


def hybrid_layer_kernel(nc, A, O):
    fp32 = mybir.dt.float32
    f32r = mybir.dt.float32r
    i32 = mybir.dt.int32
    ALU = mybir.AluOpType
    ACT = mybir.ActivationFunctionType
    AX = mybir.AxisListType

    P = 128
    NM = A["meta"].shape[0]
    SEQ, D = A["x_prompt"].shape[1:]
    NB = A["x_sample"].shape[0]
    TP = NM + SEQ
    NT = TP + NB
    DA = A["state_lru"].shape[2]
    HB, DK, DV = A["state_gla"].shape[2:]
    GR = A["w_gate_up"].shape[1]
    NE, FF = A["w_gu"].shape[1], A["w_down"].shape[2]
    EPS = 1e-6
    CH = 64
    SB = 16
    NCH = SEQ // CH
    NSB = CH // SB
    KD = D // P
    MA = DA // P
    HP = HB // 2
    TC = 3
    TL = NT - 2 * P
    NF = 2 * FF // P
    C_RG, TAU, TOPK = 8.0, 16.0, 4
    ALPHA, LIMIT = 1.702, 7.0
    CLAMP = 40.0
    S = 64
    NV = NE * -(-NT // S)

    NPIECE = 12
    NATIVE = (2, 9)
    GU = list(range(8))
    DN = list(range(8, 12))
    split_gu = [p for p in GU if p not in NATIVE]
    split_dn = [p for p in DN if p not in NATIVE]
    ring_slot = {(p, q): 2 * (n % 2) + q for n, p in enumerate(split_gu + split_dn) for q in range(2)}
    assert len(split_gu + split_dn) % 2 == 0
    TURNS = len(split_gu) % 2 == 1

    def order(p, n, ahead=True, q=1):
        ng, nd = 2 * len(split_gu), 2 * len(split_dn)
        if p in GU:
            before = 0 if isinstance(n, int) and n == 0 else n * (ng + nd) - nd
            return before + 2 * split_gu.index(p) + q + 1
        return (n + 1) * (ng + nd) - nd + (ng if ahead else 0) + 2 * split_dn.index(p) + q + 1

    ctx = ExitStack()
    with ctx:
        sems = {}

        def sem(name):
            if name not in sems:
                sems[name] = ctx.enter_context(nc.semaphore(name))
            return sems[name]

        def sb(stack, name, shape, dt=fp32):
            return stack.enter_context(nc.sbuf_tensor(name, shape, dt))

        raw = sb(ctx, "raw", [P, NPIECE, 2048])
        yacc = sb(ctx, "yacc", [P, TC, D])
        ident = sb(ctx, "ident", [P, P])
        slot_no = sb(ctx, "slot_no", [P, 2 * S])
        ones = sb(ctx, "ones", [P, P])
        pv = sb(ctx, "pv", [P, 47])
        bguT = sb(ctx, "bguT", [P, NF, NE])
        pos = sb(ctx, "pos", [P, TC, NV + 2])
        gate = sb(ctx, "gate", [P, TC, NV])
        small = sb(ctx, "small", [P, 112])
        flag = sb(ctx, "flag", [P, 1], i32)
        G_MIX, CONV_W, CONV_B, BRA, BRX, LAM, GNA, BGATE, GNB = 0, 8, 24, 28, 32, 36, 40, 44, 46

        mx = ExitStack()
        wv = sb(mx, "wv", [P, 3, KD, 512])
        uT = sb(mx, "uT", [P, KD, NT])
        proj = sb(mx, "proj", [P, 20, NT])
        wlr = sb(mx, "wlr", [P, KD, GR])
        gup = sb(mx, "gup", [GR, HB * DK])
        lrT = sb(mx, "lrT", [GR, NT])
        seg = sb(mx, "seg", [P, NT])
        cm = sb(mx, "cm", [CH, CH])
        spare = sb(mx, "spare", [P, 2, MA, NT])
        mx.close()

        me = ExitStack()
        uhi = sb(me, "uhi", [P, TC, D], f32r)
        ulo = sb(me, "ulo", [P, TC, D], f32r)
        ringhi = sb(me, "ringhi", [P, 4, 1024], f32r)
        ringlo = sb(me, "ringlo", [P, 4, 1024], f32r)
        xT = sb(me, "xT", [P, KD, 2 * S], f32r)
        actT = sb(me, "actT", [P, KD, 2 * S], f32r)
        selz = sb(me, "selz", [P, TC, 3 * S], f32r)
        xr = sb(me, "xr", [P, D])
        Gm = sb(me, "Gm", [P, TC, 2 * S])
        GT = sb(me, "GT", [P, TC * P])
        guS = sb(me, "guS", [S, 2048])
        yS = sb(me, "yS", [P, D])
        hS = sb(me, "hS", [P, 2, 8 * S])
        sig = sb(me, "sig", [P, 8 * S])
        me.close()
        ps = ctx.enter_context(nc.psum_tensor("ps", [P, 8, 512], fp32))

        def flat(a):
            return a.rearrange("p a n -> p (a n)")

        wqk = flat(raw[:, 8:10, :]).rearrange("p (k n) -> p k n", n=512)
        wvv = flat(raw[:, 10:12, :]).rearrange("p (k n) -> p k n", n=512)
        wout = wv[:, 1:3].rearrange("p a k n -> p (a k n)").rearrange("p (k n) -> p k n", n=D)

        class Area:

            def __init__(self, ap):
                self.ap, self.at = ap, 0

            def cut(self, *dims):
                n = 1
                for d in dims:
                    n *= d
                got = self.ap[:, self.at:self.at + n]
                self.at += n
                assert self.at <= self.ap.shape[1]
                if len(dims) == 2:
                    got = got.rearrange("p (a b) -> p a b", a=dims[0])
                elif len(dims) == 3:
                    got = got.rearrange("p (a b c) -> p a b c", a=dims[0], b=dims[1])
                return got

        early = Area(flat(raw[:, 4:8, :]))
        cs = early.cut(MA, 32)
        la = early.cut(HP, NT)
        bc = early.cut(HP, NT)
        ta = early.cut(HP, NT)
        qI = early.cut(HP, NT)
        qE = early.cut(HP, NT)
        kD = early.cut(HP, TP)
        kI = early.cut(HP, NSB, SEQ)
        kIl = early.cut(HP, NM)
        PT = early.cut(NCH + 1, HB, CH)
        XW = TP + 3
        xp = early.cut(MA, XW)
        assert early.at <= 4 * 2048
        first = Area(flat(raw[:, 4:8, :]))
        first.cut(MA, 32)
        xn = first.cut(TC, D)
        pin = first.cut(P)
        cst = first.cut(DA)
        bgr = first.cut(2 * FF)
        Sg = [flat(la)[:, n * HP * DV:(n + 1) * HP * DV].rearrange("p (a v) -> p a v", a=HP) for n in range(2)]
        second = Area(flat(raw[:, 8:10, :]))
        VT = second.cut(NCH + 1, HB * DV)
        KT = second.cut(NCH + 1, HB * DK)
        third = Area(flat(raw[:, 10:12, :]))
        xc = third.cut(MA, NT)
        rr = third.cut(MA, NT)
        ii = third.cut(MA, NT)
        vs = third.cut(HB * DV)
        aa, tt = spare[:, 0], spare[:, 1]
        S0 = flat(wv[:, 0])[:, 0:2048].rearrange("p (b a v) -> p b a v", b=NB, a=HP)
        Sn = flat(wv[:, 0])[:, 2048:4096].rearrange("p (b a v) -> p b a v", b=NB, a=HP)
        kflat = kI.rearrange("p a b n -> p (a b n)")
        T2 = kflat[:, 0:MA * NT].rearrange("p (m n) -> p m n", m=MA)
        NO = 3 + NB + 1 + NB
        OT = kflat[:, 1120:1120 + MA * NO].rearrange("p (m n) -> p m n", m=MA)
        OS = kflat[0:NO, 1280:1280 + DA]
        T3 = early.ap[:, 1808:1808 + MA * NT].rearrange("p (m n) -> p m n", m=MA)
        eS = small[:, 24:24 + HP * NB].rearrange("p (a b) -> p a b", a=HP)
        qS = [small[:, n:n + HP * NB].rearrange("p (a b) -> p a b", a=HP) for n in (40, 93)]
        qE = [qE, ta]
        eb = small[:, 56:56 + HP * (NCH + 1)].rearrange("p (a c) -> p a c", a=HP)
        ssq, rstd = small[:, 0:3], small[:, 4:7]
        nsp8, la0, la1, la2 = (small[:, 8 + 4 * n:12 + 4 * n] for n in range(4))
        WA = flat(tt)[:, 0:MA * P].rearrange("p (m n) -> p m n", m=MA)
        WX = flat(tt)[:, MA * P:2 * MA * P].rearrange("p (m n) -> p m n", m=MA)
        u2 = flat(raw[:, 8:10, :])[:, 0:TC * D].rearrange("p (c d) -> p c d", c=TC)
        rt = Area(flat(raw[:, 8:10, :]))
        rt.cut(TC * D)
        wr = rt.cut(KD, NE)
        brow = rt.cut(NE)
        lg = rt.cut(TC, NE)
        em = rt.cut(TC, NE)
        mk = rt.cut(TC, NE)
        eq = rt.cut(TC, NE)
        gtv = rt.cut(TC, NE)
        u2T = flat(raw[:, 10:12, :])[:, 0:KD * TC * P].rearrange("p (k t) -> p k t", k=KD)
        gff = flat(raw[:, 10:12, :])[:, 3072:4096]
        tri = sig[:, 0:P]
        valid = small[:, 90:93]
        bdn = yS[0:NE, :]
        GTd = GT[0:NE, :]
        gfin = flat(raw[:, 0:1, :])[:, 0:D]
        yout = flat(raw[:, 1:3, :])[:, 0:TC * D].rearrange("p (c d) -> p c d", c=TC)
        junk = raw[:, 4, 0:D]

        chunks = [(0, NM)] + [(NM + CH * c, CH) for c in range(NCH)]
        rows_of = [P, P, TL]

        x = A["x_prompt"]
        block = ctx.enter_context(nc.Block())

        def projections():
            yield "in_lr", lambda k: wlr[:, k, :], GR
            for name, w in (("in_qk", wqk), ("in_v", wvv), ("in_xa", wv[:, 0]), ("in_ya", wv[:, 1]), ("in_g", wv[:, 2])):
                for m in range(4):
                    yield name, (lambda k, w=w, m=m: w[:, k, m * P:(m + 1) * P]), P

        TILES = list(projections())
        N_XA = 13
        VTILES = (5, 6, 7, 8)

        def evacuator(t):
            act = [n for n in range(len(TILES)) if n in VTILES or n >= N_XA]
            return ("proj_act", act.index(t) + 1) if t in act else ("proj_dve", t + 1 - sum(n < t for n in act))

        def e_of(i):
            return i if isinstance(i, int) else i % NE

        @block.sync
        def _(sp):
            def load(dst, src, name):
                sp.dma_start(dst, src).then_inc(sem(name), 16)

            load(yacc[0:NM, 0, :], A["meta"], "x_in")
            load(yacc[NM:P, 0, :], x[0, 0:P - NM, :], "x_in")
            load(yacc[:, 1, :], x[0, P - NM:2 * P - NM, :], "x_in")
            sp.wait_ge(sem("tail_zero"), 1)
            load(yacc[0:TP - 2 * P, 2, :], x[0, 2 * P - NM:SEQ, :], "x_in")
            load(yacc[TP - 2 * P:TL, 2, :], A["x_sample"][:, 0, :], "x_in")
            win = A["w_in"][0].rearrange("(k p) n -> p k n", p=P)
            load(wlr[:, :, :], win[:, :, 2560:2576], "in_lr")
            load(wqk, win[:, :, 2 * DA:2 * DA + 512], "in_qk")
            load(gup[:, :], A["w_gate_up"][0], "gup_in")
            load(wvv, win[:, :, 1536:2048], "in_v")
            load(wv[:, 0], win[:, :, 0:512], "in_xa")
            load(wv[:, 1], win[:, :, 512:1024], "in_ya")
            load(wv[:, 2], win[:, :, 2048:2560], "in_g")
            for p in range(4):
                load(raw[:, p, :], A["w_gu"][0, 0, p * P:(p + 1) * P, :], f"piece_in{p}")
            sp.wait_ge(sem("proj_done"), N_XA)
            for b in range(NB):
                load(S0[:, b], A["state_gla"][0, b].rearrange("(a h) k v -> (h k) a v", h=2), "s0_in")
            sp.wait_ge(sem("proj_done"), len(TILES))
            load(wout, A["w_out"][0].rearrange("(k p) n -> p k n", p=P), "wout_in")
            sp.wait_ge(sem("gla_state"), NCH + 1)
            sp.dma_start(O["gla_p"][0, 0].rearrange("(a h) k v -> (h k) a v", h=2), Sg[NCH % 2]).then_inc(sem("out_mix"), 16)
            sp.wait_ge(sem("sample_state"), 1)
            for b in range(NB):
                sp.dma_start(O["gla_s"][0, b].rearrange("(a h) k v -> (h k) a v", h=2), Sn[:, b]).then_inc(sem("out_mix"), 16)
            sp.wait_ge(sem("rows_ready"), 1)
            sp.dma_start(O["conv_p"][0, 0], OS[0:3, :]).then_inc(sem("out_mix"), 16)
            sp.dma_start(O["conv_s"][0, :, 0:2, :], A["state_conv"][0, :, 1:3, :]).then_inc(sem("out_mix"), 16)
            sp.dma_start(O["conv_s"][0, :, 2, :], OS[3:3 + NB, :]).then_inc(sem("out_mix"), 16)
            sp.dma_start(O["lru_p"][0], OS[3 + NB:4 + NB, :]).then_inc(sem("out_mix"), 16)
            sp.dma_start(O["lru_s"][0], OS[4 + NB:NO, :]).then_inc(sem("out_mix"), 16)
            sp.wait_ge(sem("out_mix"), 16 * (1 + NB + 5))
            sp.wait_ge(sem("h_ready"), 6)
            load(gff, A["g_ffn"].broadcast_to([P, D]), "router_in")
            load(wr, A["w_router"][0].rearrange("(k p) e -> p k e", p=P), "router_in")
            load(brow[0:1, :], A["b_router"], "router_in")
            load(bdn, A["b_down"][0], "router_in")

            def piece(p, i, first=False):
                if not first:
                    if p in NATIVE:
                        sp.wait_ge(sem(f"native_used{p}"), i)
                    else:
                        sp.wait_ge(sem("hi_made"), order(p, i - 1))
                        sp.wait_ge(sem("lo_made"), order(p, i - 1))
                e = e_of(i)
                if p in GU:
                    src = A["w_gu"][0, bass.ds(e, 1), p * P:(p + 1) * P, :].rearrange("e p n -> (e p) n")
                    load(raw[:, p, :], src, f"piece_in{p}")
                else:
                    r = (p - 8) * 2 * P
                    src = A["w_down"][0, bass.ds(e, 1), r:r + 2 * P, :].rearrange("e (k p) n -> p (e k) n", p=P)
                    load(raw[:, p, :].rearrange("p (k n) -> p k n", k=2), src, f"piece_in{p}")

            for p in range(4, 8):
                piece(p, 0, first=True)
            sp.wait_ge(sem("pos_ready"), 1)
            for p in GU:
                piece(p, 1)
            for p in DN:
                piece(p, 0, first=True)
            with sp.Fori(2, NE) as i:
                for p in GU:
                    piece(p, i)
                for p in DN:
                    piece(p, i - 1)
            sp.wait_ge(sem("flag_ready"), 1)
            over = sp.value_load(flag[0:1, 0:1], min_val=0, max_val=1)
            last = over * (NV - NE) + NE
            with sp.If(over):
                with sp.Fori(NE, NV) as i:
                    for p in GU:
                        piece(p, i)
                    for p in DN:
                        piece(p, i - 1)
            for p in DN:
                if p in NATIVE:
                    sp.wait_ge(sem(f"native_used{p}"), last - 1)
                else:
                    sp.wait_ge(sem("hi_made"), order(p, last - 2))
                    sp.wait_ge(sem("lo_made"), order(p, last - 2))
                r = (p - 8) * 2 * P
                load(raw[:, p, :].rearrange("p (k n) -> p k n", k=2),
                     A["w_down"][0, NE - 1, r:r + 2 * P, :].rearrange("(k p) n -> p k n", p=P), f"piece_in{p}")
            sp.wait_ge(sem("split_used"), order(7, last - 1))
            load(gfin, A["g_final"].rearrange("(a n) -> a n", a=1).broadcast_to([P, D]), "gfin_in")
            sp.wait_ge(sem("y_ready"), 1)
            sp.dma_start(O["y_p"][0, 0:P - NM, :], yout[NM:P, 0, :]).then_inc(sem("out_y"), 16)
            sp.wait_ge(sem("y_ready"), 2)
            sp.dma_start(O["y_p"][0, P - NM:2 * P - NM, :], yout[:, 1, :]).then_inc(sem("out_y"), 16)
            sp.wait_ge(sem("y_ready"), 3)
            sp.dma_start(O["y_p"][0, 2 * P - NM:SEQ, :], yout[0:TP - 2 * P, 2, :]).then_inc(sem("out_y"), 16)
            sp.dma_start(O["y_s"][:, 0, :], yout[TP - 2 * P:TL, 2, :]).then_inc(sem("out_y"), 16)
            sp.wait_ge(sem("out_y"), 64)

        def passes(eng, body, load_flag=True):
            body(0)
            body(1)
            with eng.Fori(2, NE) as i:
                body(i)
            eng.wait_ge(sem("flag_ready"), 1)
            over = eng.value_load(flag[0:1, 0:1], min_val=0, max_val=1)
            with eng.If(over):
                with eng.Fori(NE, NV) as i:
                    body(i)
            last = over * (NV - NE) + NE
            body(last, ahead=False)
            body(last + 1, ahead=False, between=False)
            return last

        def lags(i, ahead, between):
            n = i if isinstance(i, int) else NE
            return ahead, between and n >= 1, n >= 2

        def ring_free(eng, p, n, ahead, q):
            turn = (p == split_gu[0] and isinstance(n, int) and n == 1) or (p == split_dn[0] and not ahead)
            at = order(p, n, ahead, q) - (2 if turn and TURNS else 4)
            if not isinstance(at, int) or at > 0:
                eng.wait_ge(sem("split_used"), at)

        @block.gpsimd
        def _(pool):
            pool.memset(ident[:, :], 0.0).then_inc(sem("zeroed"), 1)
            pool.memset(ones[:, :], 1.0).then_inc(sem("zeroed"), 1)
            pool.memset(cm[:, :], 1.0).then_inc(sem("zeroed"), 1)
            pool.memset(WA, 0.0).then_inc(sem("zeroed"), 1)
            pool.memset(WX, 0.0).then_inc(sem("zeroed"), 1)
            pool.wait_ge(sem("zeroed"), 5)
            pool.affine_select(out=ident[:, :], in_=ident[:, :], compare_op=ALU.not_equal, fill=1.0,
                               base=0, pattern=[[-1, P]], channel_multiplier=1).then_inc(sem("ident_ready"), 1)
            pool.affine_select(out=cm[:, :], in_=cm[:, :], compare_op=ALU.is_ge, fill=0.0,
                               base=0, pattern=[[1, CH]], channel_multiplier=-1).then_inc(sem("cm_ready"), 1)
            pool.iota(slot_no[:, :].rearrange("p (a s) -> p a s", a=2), pattern=[[0, 2], [1, S]], base=0,
                      channel_multiplier=0, allow_small_or_imprecise_dtypes=True).then_inc(sem("slot_no_ready"), 1)
            for m in range(MA):
                for h in range(2):
                    r = slice(64 * h, 64 * h + 64)
                    pool.dma_start(WA[r, m, 64 * h:64 * h + 64], A["w_rg_a"][0, 2 * m + h]).then_inc(sem("wrg_in"), 16)
                    pool.dma_start(WX[r, m, 64 * h:64 * h + 64], A["w_rg_x"][0, 2 * m + h]).then_inc(sem("wrg_in"), 16)
            pool.wait_ge(sem("h_ready"), 6)
            pool.memset(sig[:, 0:P], 1.0).then_inc(sem("pool_own"), 1)
            pool.memset(valid, 1.0).then_inc(sem("pool_own"), 1)
            pool.wait_ge(sem("pool_own"), 2)
            pool.affine_select(out=tri, in_=tri, compare_op=ALU.is_ge, fill=0.0, base=-1,
                               pattern=[[1, P]], channel_multiplier=-1).then_inc(sem("tri_ready"), 1)
            pool.affine_select(out=valid, in_=valid, compare_op=ALU.is_ge, fill=0.0, base=NT - 1,
                               pattern=[[-P, TC]], channel_multiplier=-1).then_inc(sem("tri_ready"), 1)
            def body(i, ahead=True, between=True):
                if between and lags(i, ahead, between)[1]:
                    pool.wait_ge(sem("gm_hot"), i)
                    pool.tensor_tensor(Gm[:, :, :], Gm[:, :, :], gate[:, :, bass.ds(i - 1, 1)].broadcast_to([P, TC, 2 * S]),
                                       ALU.mult).then_inc(sem("gm_ready"), 1)

            pool.wait_ge(sem("pos_ready"), 1)
            passes(pool, body)

        @block.scalar
        def _(act):
            chain = [0]

            def link(ins):
                chain[0] += 1
                ins.then_inc(sem("act_chain"), 1)
                act.wait_ge(sem("act_chain"), chain[0])

            def row(dst, src, name="par_in"):
                act.dma_start(dst, src).then_inc(sem(name), 16)

            def by_tile(ap):
                return ap.rearrange("a (r c) -> (a r) c", c=P)

            row(pin[0:8, :], by_tile(A["g_mix"]))
            row(pin[8:24, :], by_tile(A["conv_w"][0]))
            row(pin[24:28, :], by_tile(A["conv_b"]))
            row(pin[28:32, :], by_tile(A["b_rg_a"]))
            row(pin[32:36, :], by_tile(A["b_rg_x"]))
            row(pin[36:40, :], by_tile(A["lam"]))
            row(pin[40:44, :], by_tile(A["gn_a"]))
            row(pin[44:46, :], by_tile(A["b_gate"]))
            row(pin[46:47, :], A["gn_b"])
            row(cst[0:24, :], A["state_conv"][0].rearrange("b j n -> (b j) n"))
            row(cst[24:32, :], A["state_lru"][0])
            row(bgr[0:NE, :], A["b_gu"][0])
            act.wait_ge(sem("x_in"), 80)
            for c in range(TC):
                act.activation(xn[:, c, :], yacc[:, c, :], ACT.Square, accum_out=ssq[:, c:c + 1]).then_inc(sem("ssq"), 1)
            act.wait_ge(sem("var"), 1)
            act.activation(rstd, ssq, ACT.Sqrt).then_inc(sem("std"), 1)
            act.wait_ge(sem("lam_abs"), 1)
            act.activation(la1, la0, ACT.Exp, scale=-1.0).then_inc(sem("lam_exp"), 1)
            act.wait_ge(sem("z_abs"), 1)
            link(act.activation(bc, bc, ACT.Exp, scale=-1.0))
            act.activation(bc, bc, ACT.Ln, bias=1.0).then_inc(sem("z_log"), 1)
            for t in VTILES:
                act.wait_ge(sem("proj_done"), t + 1)
                act.activation(proj[:, t - 1, :], ps[:, t % 4, 0:NT], ACT.Copy).then_inc(sem("proj_act"), 1)
            act.wait_ge(sem("shifted"), 1)
            act.activation(eb, bc[:, :, NM - 1:TP:CH], ACT.Exp).then_inc(sem("decays"), 1)
            act.activation(eS, bc[:, :, TP:NT], ACT.Exp).then_inc(sem("decays"), 1)
            act.activation(qE[0], bc, ACT.Exp).then_inc(sem("decays"), 1)
            act.activation(qI[:, :, 0:TP], ta[:, :, 0:TP], ACT.Exp).then_inc(sem("decays"), 1)
            act.wait_ge(sem("shifted"), 2)
            act.activation(kI.rearrange("p a b n -> p (a b n)"), kI.rearrange("p a b n -> p (a b n)"), ACT.Exp).then_inc(sem("decays"), 1)
            act.activation(kIl, kIl, ACT.Exp).then_inc(sem("decays"), 1)
            act.activation(kD, kD, ACT.Exp).then_inc(sem("decays"), 1)
            for c, (t0, n) in enumerate(chunks):
                act.wait_ge(sem("turned"), c + 1)
                act.activation(VT[0:n, c, :], ps[0:n, 6, :], ACT.Copy).then_inc(sem("vt"), 1)
                act.activation(KT[0:n, c, :], ps[0:n, 7, 0:HB * DK], ACT.Copy).then_inc(sem("vt"), 1)
            for t in range(13, 17):
                act.wait_ge(sem("proj_done"), t + 1)
                act.activation(proj[:, t - 1, :], ps[:, t % 4, 0:NT], ACT.Gelu_apprx_tanh).then_inc(sem("proj_act"), 1)
            for m in range(MA):
                act.wait_ge(sem("rg_done"), 2 * m + 1)
                act.activation(rr[:, m, :], ps[:, 6, 0:NT], ACT.Sigmoid, bias=pv[:, BRA + m:BRA + m + 1]).then_inc(sem("rg_sig"), 1)
                act.wait_ge(sem("rg_done"), 2 * m + 2)
                act.activation(ii[:, m, :], ps[:, 7, 0:NT], ACT.Sigmoid, bias=pv[:, BRX + m:BRX + m + 1]).then_inc(sem("rg_sig"), 1)
            for t in range(17, 21):
                act.wait_ge(sem("proj_done"), t + 1)
                act.activation(proj[:, t - 1, :], ps[:, t % 4, 0:NT], ACT.Silu).then_inc(sem("proj_act"), 1)
            act.wait_ge(sem("log_a"), 1)
            act.activation(aa, rr, ACT.Exp).then_inc(sem("a_ready"), 1)
            act.activation(tt, rr, ACT.Tanh, scale=-1.0).then_inc(sem("a_ready"), 1)
            act.wait_ge(sem("om"), 1)
            act.activation(tt, tt, ACT.Sqrt, scale=2.0).then_inc(sem("om_root"), 1)
            act.wait_ge(sem("var_a"), 1)
            act.activation(aa[:, 0, :], aa[:, 0, :], ACT.Sqrt).then_inc(sem("std_a"), 1)
            act.wait_ge(sem("o_done"), 1)
            act.activation(tt, ps[:, 0:HB, 0:NT], ACT.Square).then_inc(sem("o_sq"), 1)
            act.wait_ge(sem("var_b"), 1)
            act.activation(T3, T3, ACT.Sqrt).then_inc(sem("std_b"), 1)
            for c in range(TC):
                act.wait_ge(sem("h_ready"), 2 * c + 2)
                if c == 0:
                    act.wait_ge(sem("out_mix"), 16 * (1 + NB + 5))
                act.activation(u2[:, c, :], yacc[:, c, :], ACT.Square, accum_out=ssq[:, c:c + 1]).then_inc(sem("ssq"), 1)
            act.wait_ge(sem("var"), 2)
            act.activation(rstd, ssq, ACT.Sqrt).then_inc(sem("std"), 1)
            for c in range(TC):
                act.wait_ge(sem("u2_ready"), c + 1)
                act.activation(uhi[:, c, :], u2[:, c, :], ACT.Copy).then_inc(sem("uhi_ready"), 1)
            for n in range(6):
                act.wait_ge(sem("u2_turned"), n + 1)
                act.activation(u2T[:, 4 * (n % 2):4 * (n % 2) + 4, (n // 2) * P:(n // 2 + 1) * P],
                               ps[:, n, :].rearrange("p (k t) -> p k t", k=4), ACT.Copy).then_inc(sem("u2T_ready"), 1)
            act.wait_ge(sem("lg_shift"), 1)
            act.activation(em, em, ACT.Exp).then_inc(sem("lg_exp"), 1)
            act.wait_ge(sem("gd_turned"), 1)
            act.activation(GTd, ps[0:NE, 0, 0:TC * P], ACT.Copy).then_inc(sem("gd_ready"), 1)

            def gathered_rows(n):
                act.wait_ge(sem("gathered"), n + 1)
                act.activation(yS[:, :].rearrange("p (a n) -> p a n", a=2), ps[:, 6:8, :], ACT.Copy).then_inc(sem("xr_ready"), 1)

            def turned_rows(n):
                act.wait_ge(sem("x_turned"), n + 1)
                if not isinstance(n, int) or n >= 1:
                    act.wait_ge(sem("split_used"), order(7, n - 1))
                act.activation(xT[:, :, :], ps[:, 6:8, :].rearrange("p a (k s) -> p (a k) s", k=4), ACT.Copy).then_inc(sem("xT_ready"), 1)

            act.wait_ge(sem("bd_done"), 6)
            gathered_rows(0)
            turned_rows(0)

            def body(i, ahead=True, between=True):
                do_i, do_j, do_m = lags(i, ahead, between)
                static = isinstance(i, int)

                def hi(p, n):
                    if p in NATIVE:
                        return
                    act.wait_ge(sem(f"piece_in{p}"), 16 * n + 16)
                    for q in range(2):
                        ring_free(act, p, n, ahead, q)
                        act.activation(ringhi[:, ring_slot[p, q], :], raw[:, p, q * 1024:(q + 1) * 1024], ACT.Copy).then_inc(sem("hi_made"), 1)

                def low_rows(n):
                    if n == 0:
                        act.wait_ge(sem("split_used"), order(7, i))
                        if not static or i >= 1:
                            act.wait_ge(sem("guS_ready"), 2 * i)
                    else:
                        act.wait_ge(sem("guS_ready"), 2 * i + 1)
                    act.activation(xr[0:S, :].rearrange("p (a n) -> p a n", a=2), ps[S:2 * S, 2 * n:2 * n + 2, :], ACT.Copy).then_inc(sem("low_ready"), 1)

                if do_i:
                    hi(0, i)
                if do_m:
                    act.wait_ge(sem("split_used"), order(11, i - 2, do_j))
                    if not static or i >= 3:
                        act.wait_ge(sem("scattered"), 6 * (i - 2))
                    if do_i:
                        act.wait_ge(sem("x_turned"), i + 1)
                    act.activation(yS[:, :].rearrange("p (a n) -> p a n", a=2), ps[:, 4:6, :], ACT.Copy).then_inc(sem("yS_ready"), 1)
                if do_i:
                    hi(1, i)
                if do_m:
                    act.wait_ge(sem("gt_turned"), i - 1)
                    act.activation(GT[:, :], ps[:, 6 if do_i else 0, 0:TC * P], ACT.Copy).then_inc(sem("gt_ready"), 1)
                if do_i:
                    hi(2, i)
                    hi(3, i)
                if do_j:
                    act.wait_ge(sem("clipped"), i)
                    act.activation(sig[:, :], hS[:, 0, :], ACT.Sigmoid, scale=ALPHA).then_inc(sem("sig_ready"), 1)
                if do_i:
                    hi(4, i)
                if do_j:
                    act.wait_ge(sem("acted"), i)
                    if not static or i >= 2:
                        act.wait_ge(sem("split_used"), order(11, i - 2))
                    act.activation(actT[:, :, 0:S], sig[:, :].rearrange("p (k s) -> p k s", k=KD), ACT.Copy).then_inc(sem("act_hi"), 1)
                if do_i:
                    for p in (5, 6, 7):
                        hi(p, i)
                if do_j:
                    hi(8, i - 1)
                if do_i:
                    gathered_rows(i + 1)
                    low_rows(0)
                if do_j:
                    hi(9, i - 1)
                    hi(10, i - 1)
                if do_i:
                    turned_rows(i + 1)
                    low_rows(1)
                if do_j:
                    hi(11, i - 1)

            last = passes(act, body)
            act.wait_ge(sem("added"), 6 * last + 6)
            for c in range(TC):
                act.activation(junk, yacc[:, c, :], ACT.Square, accum_out=ssq[:, c:c + 1]).then_inc(sem("ssq"), 1)
                act.wait_ge(sem("ssq"), 2 * TC + c + 1)
            act.wait_ge(sem("var"), 3)
            act.activation(rstd, ssq, ACT.Sqrt).then_inc(sem("std"), 1)

        @block.vector
        def _(dve):
            chain = [0]

            def link(*many):
                for ins in many:
                    chain[0] += 1
                    ins.then_inc(sem("dve_chain"), 1)
                dve.wait_ge(sem("dve_chain"), chain[0])

            dve.memset(yacc[:, 2, :], 0.0).then_inc(sem("tail_zero"), 1)
            link(dve.memset(seg[:, :], 1.0), dve.memset(xp[:, :, 0:3], 0.0))
            for t0, _ in chunks:
                dve.memset(seg[:, t0:t0 + 1], 0.0).then_inc(sem("seg_ready"), 1)
            dve.memset(seg[:, TP:NT], 0.0).then_inc(sem("seg_ready"), 1)
            dve.wait_ge(sem("par_turned"), 1)
            dve.tensor_copy(pv[:, :], ps[:, 0, 0:47]).then_inc(sem("par_ready"), 1)
            dve.tensor_copy(cs, ps[:, 1, 0:MA * 32].rearrange("p (m n) -> p m n", m=MA)).then_inc(sem("par_ready"), 1)
            dve.tensor_copy(bguT[:, :, :], ps[:, 2, :].rearrange("p (f e) -> p f e", f=NF)).then_inc(sem("par_ready"), 1)
            dve.wait_ge(sem("ssq"), TC)
            dve.tensor_scalar(ssq, ssq, 1.0 / D, EPS, ALU.mult, ALU.add).then_inc(sem("var"), 1)
            dve.wait_ge(sem("std"), 1)
            link(dve.reciprocal(rstd, rstd))
            for c in range(TC):
                dve.tensor_scalar(xn[:, c, :], yacc[:, c, :], rstd[:, c:c + 1], None, ALU.mult).then_inc(sem("xn_ready"), 1)
            dve.wait_ge(sem("par_ready"), 3)
            for k in range(KD):
                dve.wait_ge(sem("u_turned"), k + 1)
                dve.tensor_scalar(uT[:, k, :], ps[:, k, 0:NT], pv[:, G_MIX + k:G_MIX + k + 1], None, ALU.mult).then_inc(sem("uT_ready"), 1)
            lam = pv[:, LAM:LAM + MA]
            dve.scalar_tensor_tensor(out=la0, in0=lam, scalar=-1.0, in1=lam, op0=ALU.mult, op1=ALU.max).then_inc(sem("lam_abs"), 1)

            def take(t):
                dve.wait_ge(sem("proj_done"), t + 1)
                if t == 0:
                    dve.tensor_copy(lrT[:, :], ps[0:GR, 0, 0:NT]).then_inc(sem("proj_dve"), 1)
                else:
                    dve.tensor_copy(proj[:, t - 1, :], ps[:, t % 4, 0:NT]).then_inc(sem("proj_dve"), 1)

            for t in range(5):
                take(t)
            for a in range(HP):
                dve.wait_ge(sem("z_done"), a + 1)
                link(dve.tensor_scalar(la[:, a, :], ps[:, 4 + a, 0:NT], pv[:, BGATE + a:BGATE + a + 1], None, ALU.add))
            dve.scalar_tensor_tensor(out=bc, in0=la, scalar=-1.0, in1=la, op0=ALU.mult, op1=ALU.max).then_inc(sem("z_abs"), 1)
            link(dve.tensor_scalar(ta, la, 0.0, 1.0 / TAU, ALU.min, ALU.mult))
            dve.wait_ge(sem("z_log"), 1)
            link(dve.scalar_tensor_tensor(out=la, in0=bc, scalar=-1.0 / TAU, in1=ta, op0=ALU.mult, op1=ALU.add))
            dve.wait_ge(sem("seg_ready"), NCH + 2)
            link(*[dve.tensor_tensor_scan(out=bc[:, a, :], data0=seg[:, :], data1=la[:, a, :], initial=0.0,
                                          op0=ALU.mult, op1=ALU.add) for a in range(HP)])
            for a in range(HP):
                b16 = bc[:, a, 0:TP].rearrange("p (n s) -> p n s", s=SB)
                link(dve.tensor_tensor(ta[:, a, 0:TP].rearrange("p (n s) -> p n s", s=SB), b16,
                                       b16[:, :, SB // 2 - 1:SB // 2].broadcast_to([P, TP // SB, SB]), ALU.subtract))
            dve.tensor_scalar(ta[:, :, 0:TP], ta[:, :, 0:TP], CLAMP, None, ALU.min).then_inc(sem("shifted"), 1)
            for a in range(HP):
                b64 = bc[:, a, NM:TP].rearrange("p (c s) -> p c s", s=CH)
                for i in range(NSB):
                    mid = SB * i + SB // 2 - 1
                    link(dve.tensor_tensor(kI[:, a, i, :].rearrange("p (c s) -> p c s", s=CH),
                                           b64[:, :, mid:mid + 1].broadcast_to([P, NCH, CH]), b64, ALU.subtract))
                link(dve.tensor_tensor(kD[:, a, NM:TP].rearrange("p (c s) -> p c s", s=CH),
                                       b64[:, :, CH - 1:CH].broadcast_to([P, NCH, CH]), b64, ALU.subtract))
            link(dve.tensor_tensor(kIl, bc[:, :, SB // 2 - 1:SB // 2].broadcast_to([P, HP, NM]), bc[:, :, 0:NM], ALU.subtract))
            link(dve.tensor_tensor(kD[:, :, 0:NM], bc[:, :, NM - 1:NM].broadcast_to([P, HP, NM]), bc[:, :, 0:NM], ALU.subtract))
            link(dve.tensor_scalar(kIl, kIl, CLAMP, None, ALU.min))
            kIf = kI.rearrange("p a b n -> p (a b n)")
            dve.tensor_scalar(kIf, kIf, CLAMP, None, ALU.min).then_inc(sem("shifted"), 1)
            for t in range(9, 13):
                take(t)
            qk = proj[:, 0:2, :], proj[:, 2:4, :]
            dve.wait_ge(sem("decays"), 7)
            dve.wait_ge(sem("proj_dve"), 5)
            low, up = slice(0, DK), slice(DK, 2 * DK)
            for mine, other, dst in ((up, low, qE[1]), (low, up, qE[0])):
                link(dve.scalar_tensor_tensor(out=dst[mine], in0=qk[0][mine], scalar=DK ** -0.5, in1=qE[0][mine], op0=ALU.mult, op1=ALU.mult),
                     dve.tensor_scalar(qS[0 if mine is low else 1][mine], qk[0][mine, :, TP:NT], DK ** -0.5, None, ALU.mult))
                dve.memset(dst[other], 0.0).then_inc(sem("qk_ready"), 1)
                dve.memset(qS[0 if mine is low else 1][other], 0.0).then_inc(sem("qk_ready"), 1)
            dve.scalar_tensor_tensor(out=qI[:, :, 0:TP], in0=qk[0][:, :, 0:TP], scalar=DK ** -0.5, in1=qI[:, :, 0:TP],
                                     op0=ALU.mult, op1=ALU.mult).then_inc(sem("qk_ready"), 1)
            dve.tensor_tensor(kD, kD, qk[1][:, :, 0:TP], ALU.mult).then_inc(sem("qk_ready"), 1)
            dve.tensor_tensor(kIl, kIl, qk[1][:, :, 0:NM], ALU.mult).then_inc(sem("qk_ready"), 1)
            for a in range(HP):
                dve.tensor_tensor(kI[:, a], kI[:, a], qk[1][:, a, NM:TP].unsqueeze(1).broadcast_to([P, NSB, SEQ]),
                                  ALU.mult).then_inc(sem("qk_ready"), 1)
            dve.wait_ge(sem("proj_dve"), 9)
            xa = proj[:, 8:12, :]
            w = lambda j, m: pv[:, CONV_W + 4 * j + m:CONV_W + 4 * j + m + 1]
            link(dve.tensor_copy(xp[:, :, 3:3 + TP], xa[:, :, 0:TP]))
            csv = cs[:, :, 0:24].rearrange("p m (b j) -> p m j b", j=3)
            for j in range(4):
                for m in range(MA):
                    src = xp[:, m, j:j + TP]
                    past = csv[:, m, j, :] if j < 3 else xa[:, m, TP:NT]
                    if j == 0:
                        cb = pv[:, CONV_B + m:CONV_B + m + 1]
                        link(dve.tensor_scalar(xc[:, m, 0:TP], src, w(j, m), cb, ALU.mult, ALU.add),
                             dve.tensor_scalar(xc[:, m, TP:NT], past, w(j, m), cb, ALU.mult, ALU.add))
                    else:
                        one = dve.scalar_tensor_tensor(out=xc[:, m, 0:TP], in0=src, scalar=w(j, m), in1=xc[:, m, 0:TP], op0=ALU.mult, op1=ALU.add)
                        two = dve.scalar_tensor_tensor(out=xc[:, m, TP:NT], in0=past, scalar=w(j, m), in1=xc[:, m, TP:NT], op0=ALU.mult, op1=ALU.add)
                        if j < 3:
                            link(one, two)
                        else:
                            one.then_inc(sem("xc_ready"), 1)
                            two.then_inc(sem("xc_ready"), 1)
            dve.wait_ge(sem("cm_ready"), 1)
            for c, (t0, n) in enumerate(chunks):
                dve.wait_ge(sem("scored"), c + 1)
                for half in range(2):
                    dve.tensor_tensor(PT[0:n, c, half:HB:2, 0:n],
                                      ps[0:n, 4 + 2 * (c % 2) + half, 0:128].rearrange("p (a t) -> p a t", a=HP)[:, :, 0:n],
                                      cm[0:n, 0:n].unsqueeze(1).broadcast_to([n, HP, n]), ALU.mult).then_inc(sem("masked"), 1)
            dve.wait_ge(sem("lam_exp"), 1)
            link(dve.tensor_scalar(la0, la1, 2.0, None, ALU.add))
            link(dve.reciprocal(la0, la0))
            link(dve.tensor_tensor(la0, la0, la1, ALU.mult))
            link(dve.tensor_tensor(la1, la0, la0, ALU.mult))
            link(dve.tensor_scalar(la2, la1, 1.0 / 19, 1.0 / 17, ALU.mult, ALU.add))
            for n in (15, 13, 11, 9, 7, 5, 3, 1):
                link(dve.tensor_tensor(la2, la2, la1, ALU.mult))
                link(dve.tensor_scalar(la2, la2, 1.0 / n, None, ALU.add))
            link(dve.tensor_tensor(la2, la2, la0, ALU.mult))
            link(dve.tensor_scalar(la1, lam, -1.0, 0.0, ALU.mult, ALU.max))
            link(dve.scalar_tensor_tensor(out=la2, in0=la2, scalar=2.0, in1=la1, op0=ALU.mult, op1=ALU.add))
            link(dve.tensor_scalar(nsp8, la2, -C_RG, None, ALU.mult))
            dve.wait_ge(sem("rg_sig"), 2 * MA)
            for m in range(MA):
                link(dve.tensor_scalar(rr[:, m, :], rr[:, m, :], nsp8[:, m:m + 1], None, ALU.mult))
            dve.engine_nop().then_inc(sem("log_a"), 1)
            link(dve.tensor_tensor(ii, ii, xc, ALU.mult))
            dve.wait_ge(sem("a_ready"), 2)
            link(dve.tensor_scalar(T2, tt, 1.0, None, ALU.add))
            link(dve.reciprocal(T2, T2))
            dve.tensor_tensor(tt, tt, T2, ALU.mult).then_inc(sem("om"), 1)
            for c in range(NCH + 1):
                dve.wait_ge(sem("st_done"), c + 1)
                if c >= 2:
                    dve.wait_ge(sem("o_chunk"), c)
                new, old = Sg[c % 2], Sg[(c - 1) % 2]
                if c == 0:
                    link(dve.tensor_copy(new, ps[:, 4, 0:HP * DV].rearrange("p (a v) -> p a v", a=HP)))
                else:
                    link(*[dve.scalar_tensor_tensor(out=new[:, a, :], in0=old[:, a, :], scalar=eb[:, a, c:c + 1],
                                                    in1=ps[:, 4 + c % 2, a * DV:(a + 1) * DV], op0=ALU.mult, op1=ALU.add) for a in range(HP)])
                dve.engine_nop().then_inc(sem("gla_state"), 1)
            dve.wait_ge(sem("om_root"), 1)
            link(dve.tensor_tensor(ii, ii, tt, ALU.mult))
            link(dve.tensor_tensor(T2[:, :, 0:NB], aa[:, :, TP:NT], cs[:, :, 24:32], ALU.mult))
            link(dve.tensor_tensor(rr[:, :, TP:NT], T2[:, :, 0:NB], ii[:, :, TP:NT], ALU.add),
                 *[dve.tensor_tensor_scan(out=rr[:, m, 0:TP], data0=aa[:, m, 0:TP], data1=ii[:, m, 0:TP], initial=0.0,
                                          op0=ALU.mult, op1=ALU.add) for m in range(MA)])
            dve.wait_ge(sem("vs_turned"), 1)
            dve.tensor_copy(vs[0:NB, :], ps[0:NB, 4, :]).then_inc(sem("vs_ready"), 1)
            dve.wait_ge(sem("s0_in"), 16 * NB)
            link(dve.tensor_tensor(S0, S0, eS.rearrange("p a b -> p b a").unsqueeze(3).broadcast_to([P, NB, HP, DV]), ALU.mult))
            dve.wait_ge(sem("v_spread"), 1)
            link(dve.tensor_tensor(Sn, ps[:, 4:8, :].rearrange("p q (b a v) -> p (q b) a v", b=2, a=HP),
                                   proj[:, 2:4, TP:NT].rearrange("p a b -> p b a").unsqueeze(3).broadcast_to([P, NB, HP, DV]), ALU.mult))
            dve.tensor_tensor(Sn, Sn, S0, ALU.add).then_inc(sem("sample_state"), 1)
            link(dve.tensor_copy(OT[:, :, 0:3], xa[:, :, TP - 3:TP]), dve.tensor_copy(OT[:, :, 3:3 + NB], xa[:, :, TP:NT]),
                 dve.tensor_copy(OT[:, :, 3 + NB:NO], rr[:, :, TP - 1:NT]))
            dve.engine_nop().then_inc(sem("ot_ready"), 1)
            dve.wait_ge(sem("proj_act"), 8)
            link(dve.tensor_tensor(xc, rr, proj[:, 12:16, :], ALU.mult))
            dve.tensor_tensor(T2, xc, xc, ALU.mult).then_inc(sem("a_sq"), 1)
            dve.wait_ge(sem("rows_turned"), 1)
            dve.tensor_copy(OS, ps[0:NO, 5, :]).then_inc(sem("rows_ready"), 1)
            dve.wait_ge(sem("a_sum"), 1)
            dve.tensor_scalar(aa[:, 0, :], ps[:, 6, 0:NT], 1.0 / DA, EPS, ALU.mult, ALU.add).then_inc(sem("var_a"), 1)
            dve.wait_ge(sem("std_a"), 1)
            dve.wait_ge(sem("proj_done"), len(TILES))
            link(dve.reciprocal(aa[:, 0, :], aa[:, 0, :]))
            for m in range(MA):
                dve.scalar_tensor_tensor(out=uT[:, m, :], in0=xc[:, m, :], scalar=pv[:, GNA + m:GNA + m + 1], in1=aa[:, 0, :],
                                         op0=ALU.mult, op1=ALU.mult).then_inc(sem("mix_ready"), 1)
            dve.wait_ge(sem("b_sum"), 1)
            dve.tensor_scalar(T3, ps[:, 4:8, 0:NT], 1.0 / DV, EPS, ALU.mult, ALU.add).then_inc(sem("var_b"), 1)
            dve.wait_ge(sem("std_b"), 1)
            link(dve.reciprocal(T3, T3))
            link(dve.tensor_tensor(T3, T3, ps[:, 0:4, 0:NT], ALU.mult))
            dve.wait_ge(sem("proj_act"), 12)
            dve.scalar_tensor_tensor(out=uT[:, 4:8, :], in0=T3, scalar=pv[:, GNB:GNB + 1], in1=proj[:, 16:20, :],
                                     op0=ALU.mult, op1=ALU.mult).then_inc(sem("mix_ready"), 1)
            for u in range(6):
                c, n = divmod(u, 2)
                r = rows_of[c]
                dve.wait_ge(sem("out_done"), u + 1)
                dst = yacc[0:r, c, n * 512:(n + 1) * 512]
                dve.tensor_tensor(dst, ps[0:r, u, :], dst, ALU.add).then_inc(sem("h_ready"), 1)
            dve.wait_ge(sem("ssq"), 2 * TC)
            dve.tensor_scalar(ssq, ssq, 1.0 / D, EPS, ALU.mult, ALU.add).then_inc(sem("var"), 1)
            dve.wait_ge(sem("std"), 2)
            link(dve.reciprocal(rstd, rstd))
            dve.wait_ge(sem("router_in"), 64)
            for c in range(TC):
                dve.scalar_tensor_tensor(out=u2[:, c, :], in0=yacc[:, c, :], scalar=rstd[:, c:c + 1], in1=gff,
                                         op0=ALU.mult, op1=ALU.mult).then_inc(sem("u2_ready"), 1)
            dve.wait_ge(sem("slot_no_ready"), 1)
            dve.tensor_scalar(selz[:, :, 0:S], slot_no[:, 0:S].unsqueeze(1).broadcast_to([P, TC, S]), 0.0, None, ALU.mult).then_inc(sem("selz_edges"), 1)
            dve.tensor_scalar(selz[:, :, 2 * S:3 * S], slot_no[:, 0:S].unsqueeze(1).broadcast_to([P, TC, S]), 0.0, None, ALU.mult).then_inc(sem("selz_edges"), 1)
            for c in range(TC):
                dve.wait_ge(sem("uhi_ready"), c + 1)
                dve.tensor_tensor(ulo[:, c, :], u2[:, c, :], uhi[:, c, :].bitcast(fp32), ALU.subtract).then_inc(sem("ulo_ready"), 1)
            dve.wait_ge(sem("lg_done"), 1)
            link(dve.tensor_copy(lg, ps[:, 6, 0:TC * NE].rearrange("p (c e) -> p c e", c=TC)))
            top = gtv.rearrange("p c e -> p (c e)")[:, 0:TC * 8].rearrange("p (c n) -> p c n", c=TC)
            top = small[:, 66:66 + TC * 8].rearrange("p (c n) -> p c n", c=TC)
            link(*[dve.max(top[:, c, :], lg[:, c, :]) for c in range(TC)])
            v4 = top[:, :, TOPK - 1:TOPK].broadcast_to([P, TC, NE])
            link(dve.tensor_tensor(gtv, lg, v4, ALU.is_gt), dve.tensor_tensor(eq, lg, v4, ALU.is_equal))
            dve.tensor_tensor(em, lg, top[:, :, 0:1].broadcast_to([P, TC, NE]), ALU.subtract).then_inc(sem("lg_shift"), 1)
            link(dve.tensor_reduce(out=ssq, in_=gtv, axis=AX.X, op=ALU.add))
            link(dve.tensor_scalar(ssq, ssq, -1.0, float(TOPK), ALU.mult, ALU.add))
            link(*[dve.tensor_tensor_scan(out=mk[:, c, :], data0=ones[:, 0:NE], data1=eq[:, c, :], initial=0.0,
                                          op0=ALU.mult, op1=ALU.add) for c in range(TC)])
            link(dve.tensor_tensor(mk, mk, ssq.unsqueeze(2).broadcast_to([P, TC, NE]), ALU.is_le))
            link(dve.tensor_tensor(mk, mk, eq, ALU.mult))
            link(dve.tensor_tensor(mk, mk, gtv, ALU.add))
            dve.wait_ge(sem("tri_ready"), 2)
            dve.tensor_tensor(mk, mk, valid.unsqueeze(2).broadcast_to([P, TC, NE]), ALU.mult).then_inc(sem("mask_ready"), 1)
            dve.wait_ge(sem("mask_ready"), 1)
            dve.wait_ge(sem("lg_exp"), 1)
            link(dve.tensor_tensor(em, em, mk, ALU.mult))
            link(dve.tensor_reduce(out=ssq, in_=em, axis=AX.X, op=ALU.add))
            link(dve.tensor_scalar(ssq, ssq, 1e-30, None, ALU.max))
            link(dve.reciprocal(ssq, ssq))
            dve.tensor_tensor(em, em, ssq.unsqueeze(2).broadcast_to([P, TC, NE]), ALU.mult).then_inc(sem("gates_ready"), 1)
            dve.wait_ge(sem("gates_ready"), 1)
            dve.wait_ge(sem("rank_done"), 1)
            link(dve.tensor_scalar(lg, ps[:, 7, 0:TC * NE].rearrange("p (c e) -> p c e", c=TC), 1.0, None, ALU.add))
            link(dve.tensor_tensor(lg, lg, mk, ALU.mult))
            rounds = NV // NE
            link(*[dve.tensor_scalar(pos[:, :, r * NE:(r + 1) * NE], lg, -1.0 - r * S, None, ALU.add) for r in range(rounds)],
                 dve.memset(pos[:, :, NV:NV + 2], -1.0),
                 *[dve.tensor_copy(gate[:, :, r * NE:(r + 1) * NE], em) for r in range(rounds)],
                 dve.tensor_reduce(out=la0[:, 0:1], in_=ps[:, 7, TC * NE:(TC + 1) * NE], axis=AX.X, op=ALU.max))
            dve.engine_nop().then_inc(sem("pos_ready"), 1)
            dve.tensor_scalar(flag[:, :], la0[:, 0:1], float(S), None, ALU.is_gt).then_inc(sem("flag_ready"), 1)
            for u in range(6):
                c, n = divmod(u, 2)
                dve.wait_ge(sem("bd_done"), u + 1)
                dst = yacc[:, c, n * 512:(n + 1) * 512]
                dve.tensor_tensor(dst, ps[:, u, :], dst, ALU.add).then_inc(sem("added"), 1)

            def one_hot(n):
                if not isinstance(n, int) or n >= 1:
                    dve.wait_ge(sem("gathered"), n)
                dve.tensor_tensor(selz[:, :, S:2 * S], slot_no[:, 0:S].unsqueeze(1).broadcast_to([P, TC, S]),
                                  pos[:, :, bass.ds(n, 1)].broadcast_to([P, TC, S]), ALU.is_equal).then_inc(sem("sel_ready"), 1)

            one_hot(0)
            one_hot(1)

            def body(i, ahead=True, between=True):
                do_i, do_j, do_m = lags(i, ahead, between)

                def lo(p, n, halves=(0, 1)):
                    if p in NATIVE:
                        return
                    for q in halves:
                        dve.wait_ge(sem("hi_made"), order(p, n, ahead, q))
                        ring_free(dve, p, n, ahead, q)
                        dve.tensor_tensor(ringlo[:, ring_slot[p, q], :], raw[:, p, q * 1024:(q + 1) * 1024],
                                          ringhi[:, ring_slot[p, q], :].bitcast(fp32), ALU.subtract).then_inc(sem("lo_made"), 1)

                def collect(us):
                    for u in us:
                        c, n = divmod(u, 2)
                        dve.wait_ge(sem("scattered"), 6 * (i - 2) + u + 1)
                        if u == 0:
                            dve.wait_ge(sem("added"), 6 * (i - 2) + 6)
                        dst = yacc[:, c, n * 512:(n + 1) * 512]
                        dve.tensor_tensor(dst, ps[:, 6 + u % 2, :], dst, ALU.add).then_inc(sem("added"), 1)

                if do_i:
                    lo(0, i)
                    lo(1, i)
                if do_j:
                    dve.wait_ge(sem("gu_turned"), i)
                    for n in range(2):
                        dve.tensor_tensor(hS[:, n, :].rearrange("p (k s) -> p k s", k=8), ps[:, 6 + n, :].rearrange("p (k s) -> p k s", k=8),
                                          bguT[:, 8 * n:8 * n + 8, bass.ds(e_of(i - 1), 1)].broadcast_to([P, 8, S]), ALU.add).then_inc(sem("biased"), 1)
                    dve.wait_ge(sem("biased"), 2 * i)
                    dve.tensor_scalar(hS[:, 0, :], hS[:, 0, :], LIMIT, None, ALU.min).then_inc(sem("clipped"), 1)
                    dve.tensor_scalar(hS[:, 1, :], hS[:, 1, :], LIMIT, -LIMIT, ALU.min, ALU.max).then_inc(sem("lin_clipped"), 1)
                if do_i:
                    lo(2, i)
                    lo(3, i, (0,))
                if do_j:
                    if do_m:
                        dve.wait_ge(sem("gt_turned"), i - 1)
                    dve.tensor_tensor(Gm[:, :, :], slot_no[:, :].unsqueeze(1).broadcast_to([P, TC, 2 * S]),
                                      pos[:, :, bass.ds(i - 1, 1)].broadcast_to([P, TC, 2 * S]), ALU.is_equal).then_inc(sem("gm_hot"), 1)
                    dve.wait_ge(sem("lin_clipped"), i)
                    dve.scalar_tensor_tensor(out=hS[:, 1, :], in0=hS[:, 1, :], scalar=1.0, in1=hS[:, 0, :], op0=ALU.add, op1=ALU.mult).then_inc(sem("product"), 1)
                if do_i:
                    lo(3, i, (1,))
                if do_m:
                    collect((0, 1))
                if do_j:
                    dve.wait_ge(sem("product"), i)
                    dve.wait_ge(sem("sig_ready"), i)
                    dve.tensor_tensor(sig[:, :], hS[:, 1, :], sig[:, :], ALU.mult).then_inc(sem("acted"), 1)
                if do_i:
                    lo(4, i)
                if do_m:
                    collect((2, 3))
                if do_i:
                    lo(5, i)
                if do_m:
                    collect((4, 5))
                if do_j:
                    dve.wait_ge(sem("act_hi"), i)
                    dve.tensor_tensor(actT[:, :, S:2 * S], sig[:, :].rearrange("p (k s) -> p k s", k=KD),
                                      actT[:, :, 0:S].bitcast(fp32), ALU.subtract).then_inc(sem("act_lo"), 1)
                if do_i:
                    lo(6, i)
                    lo(7, i)
                if do_j:
                    lo(8, i - 1)
                if do_i:
                    one_hot(i + 2)
                for n in range(2):
                    if do_i:
                        dve.wait_ge(sem("low_ready"), 2 * i + n + 1)
                        if n == 0 and (not isinstance(i, int) or i >= 1):
                            dve.wait_ge(sem("gu_turned"), i)
                        dve.tensor_tensor(guS[:, n * 1024:(n + 1) * 1024].rearrange("p (a n) -> p a n", a=2), ps[0:S, 2 * n:2 * n + 2, :],
                                          xr[0:S, :].rearrange("p (a n) -> p a n", a=2), ALU.add).then_inc(sem("guS_ready"), 1)
                    if do_j:
                        if n == 0:
                            lo(9, i - 1)
                        lo(10 + n, i - 1)

            passes(dve, body)
            dve.wait_ge(sem("ssq"), 3 * TC)
            dve.tensor_scalar(ssq, ssq, 1.0 / D, EPS, ALU.mult, ALU.add).then_inc(sem("var"), 1)
            dve.wait_ge(sem("std"), 3)
            link(dve.reciprocal(rstd, rstd))
            dve.wait_ge(sem("gfin_in"), 16)
            for c in range(TC):
                dve.scalar_tensor_tensor(out=yout[:, c, :], in0=yacc[:, c, :], scalar=rstd[:, c:c + 1], in1=gfin,
                                         op0=ALU.mult, op1=ALU.mult).then_inc(sem("y_ready"), 1)

        @block.tensor
        def _(pe):
            pe.wait_ge(sem("ident_ready"), 1)
            pe.wait_ge(sem("par_in"), 16 * 12)
            pe.transpose(ps[:, 0, 0:47], pin[0:47, :], ident[0:47, 0:47])
            for m in range(MA):
                pe.transpose(ps[:, 1, 32 * m:32 * m + 32], cst[0:32, m * P:(m + 1) * P], ident[0:32, 0:32])
            for f in range(NF):
                last = pe.transpose(ps[:, 2, NE * f:NE * (f + 1)], bgr[0:NE, f * P:(f + 1) * P], ident[0:NE, 0:NE])
            last.then_inc(sem("par_turned"), 1)
            pe.wait_ge(sem("xn_ready"), TC)
            pe.wait_ge(sem("par_ready"), 3)
            for k in range(KD):
                for c in range(TC):
                    r = rows_of[c]
                    last = pe.transpose(ps[:, k, c * P:c * P + r], xn[0:r, c, k * P:(k + 1) * P], ident[0:r, 0:r])
                last.then_inc(sem("u_turned"), 1)
            pe.wait_ge(sem("uT_ready"), KD)

            def project(t):
                name, w, rows = TILES[t]
                pe.wait_ge(sem(name), 16)
                if t >= 4:
                    who, n = evacuator(t - 4)
                    pe.wait_ge(sem(who), n)
                for k in range(KD):
                    last = pe.matmul(ps[0:rows, t % 4, 0:NT], w(k), uT[:, k, :], start=(k == 0), stop=(k == KD - 1))
                last.then_inc(sem("proj_done"), 1)

            for t in range(5):
                project(t)
            pe.wait_ge(sem("proj_dve"), 1)
            pe.wait_ge(sem("gup_in"), 16)
            for a in range(HP):
                pe.matmul(ps[:, 4 + a, 0:NT], gup[:, a * P:(a + 1) * P], lrT[:, :], start=True, stop=True).then_inc(sem("z_done"), 1)
            for t in range(5, 13):
                project(t)
            pe.wait_ge(sem("proj_act"), 4)
            pe.wait_ge(sem("qk_ready"), 6)
            for c, (t0, n) in enumerate(chunks):
                if c >= 1:
                    pe.wait_ge(sem("vt"), 2 * c)
                for h in range(HB):
                    pe.transpose(ps[0:n, 6, h * DV:(h + 1) * DV], proj[:, 4 + h, t0:t0 + n], ident[:, :])
                for a in range(HP):
                    last = pe.transpose(ps[0:n, 7, a * P:(a + 1) * P], kD[:, a, t0:t0 + n], ident[:, :])
                last.then_inc(sem("turned"), 1)
            for t in range(13, 17):
                project(t)
            pe.wait_ge(sem("qk_ready"), 9)
            pe.wait_ge(sem("vt"), 2 * (NCH + 1))
            for c, (t0, n) in enumerate(chunks):
                if c >= 2:
                    pe.wait_ge(sem("masked"), 2 * (c - 1))
                for h in range(HB):
                    a, r = h // 2, slice(64 * (h % 2), 64 * (h % 2) + 64)
                    for i in range(max(1, n // SB)):
                        keys = kIl[r, a, :] if c == 0 else kI[r, a, i, (c - 1) * CH:c * CH]
                        col = a * CH + SB * i
                        last = pe.matmul(ps[0:n, 4 + 2 * (c % 2) + h % 2, col:col + SB], keys,
                                         qI[r, a, t0 + SB * i:t0 + SB * (i + 1)], start=True, stop=True)
                last.then_inc(sem("scored"), 1)
            pe.wait_ge(sem("wrg_in"), 16 * 4 * MA)
            pe.wait_ge(sem("xc_ready"), 2 * MA)
            pe.wait_ge(sem("masked"), 2 * (NCH + 1))
            for m in range(MA):
                for g, wt in enumerate((WA, WX)):
                    if m:
                        pe.wait_ge(sem("rg_sig"), 2 * (m - 1) + g + 1)
                    pe.matmul(ps[:, 6 + g, 0:NT], wt[:, m, :], xc[:, m, :], start=True, stop=True).then_inc(sem("rg_done"), 1)
            for t in range(17, 21):
                project(t)
            pe.wait_ge(sem("proj_act"), 12)
            pe.wait_ge(sem("masked"), 2 * (NCH + 1))
            for c, (t0, n) in enumerate(chunks):
                if c >= 2:
                    pe.wait_ge(sem("gla_state"), c - 1)
                for h in range(HB):
                    a, o = h // 2, 64 * (h % 2)
                    last = pe.matmul(ps[o:o + 64, 4 + c % 2, a * DV:(a + 1) * DV], KT[0:n, c, h * DK:(h + 1) * DK],
                                     VT[0:n, c, h * DV:(h + 1) * DV], start=True, stop=True)
                last.then_inc(sem("st_done"), 1)
                for h in range(HB):
                    a, o = h // 2, 64 * (h % 2)
                    last = pe.matmul(ps[:, h, t0:t0 + n], VT[0:n, c, h * DV:(h + 1) * DV], PT[0:n, c, h, 0:n], start=True, stop=(c == 0))
                    if c >= 1:
                        if h == 0:
                            pe.wait_ge(sem("gla_state"), c)
                        last = pe.matmul(ps[:, h, t0:t0 + n], Sg[(c - 1) % 2][:, a, :], qE[h % 2][:, a, t0:t0 + n], start=False, stop=True)
                last.then_inc(sem("o_chunk"), 1)
            pe.wait_ge(sem("gla_state"), NCH + 1)
            for h in range(HB):
                last = pe.transpose(ps[0:NB, 4, h * DV:(h + 1) * DV], proj[:, 4 + h, TP:NT], ident[:, :])
            last.then_inc(sem("vs_turned"), 1)
            pe.wait_ge(sem("vs_ready"), 1)
            pe.wait_ge(sem("rg_sig"), 2 * MA)
            vh = vs[0:NB, :].rearrange("p (a h v) -> p a h v", a=HP, h=2)
            for b in range(NB):
                for half in range(2):
                    last = pe.matmul(ps[64 * half:64 * half + 64, 4 + b // 2, (b % 2) * 256:(b % 2) * 256 + 256],
                                     ident[0:NB, b:b + 1].broadcast_to([NB, 64]), vh[:, :, half, :], start=True, stop=True)
            last.then_inc(sem("v_spread"), 1)
            pe.wait_ge(sem("sample_state"), 1)
            for b in range(NB):
                for h in range(HB):
                    a, o = h // 2, 64 * (h % 2)
                    last = pe.matmul(ps[:, h, TP + b:TP + b + 1], Sn[:, b, a, :], qS[h % 2][:, a, b:b + 1], start=True, stop=True)
            last.then_inc(sem("o_done"), 1)
            pe.wait_ge(sem("ot_ready"), 1)
            for m in range(MA):
                last = pe.transpose(ps[0:NO, 5, m * P:(m + 1) * P], OT[:, m, :], ident[:, :])
            last.then_inc(sem("rows_turned"), 1)
            pe.wait_ge(sem("a_sq"), 1)
            for m in range(MA):
                last = pe.matmul(ps[:, 6, 0:NT], ones[:, :], T2[:, m, :], start=(m == 0), stop=(m == MA - 1))
            last.then_inc(sem("a_sum"), 1)
            pe.wait_ge(sem("o_sq"), 1)
            pe.wait_ge(sem("rows_ready"), 1)
            pe.wait_ge(sem("var_a"), 1)
            for h in range(HB):
                last = pe.matmul(ps[:, 4 + h, 0:NT], ones[:, :], tt[:, h, :], start=True, stop=True)
            last.then_inc(sem("b_sum"), 1)
            pe.wait_ge(sem("wout_in"), 16)
            pe.wait_ge(sem("mix_ready"), MA + 1)
            for u in range(6):
                c, n = divmod(u, 2)
                r = rows_of[c]
                for k in range(KD):
                    last = pe.matmul(ps[0:r, u, :], uT[:, k, c * P:c * P + r], wout[:, k, n * 512:(n + 1) * 512], start=(k == 0), stop=(k == KD - 1))
                last.then_inc(sem("out_done"), 1)
            for c in range(TC):
                pe.wait_ge(sem("u2_ready"), c + 1)
                for q in range(2):
                    for k in range(4):
                        last = pe.transpose(ps[:, 2 * c + q, k * P:(k + 1) * P], u2[:, c, (4 * q + k) * P:(4 * q + k + 1) * P], ident[:, :])
                    last.then_inc(sem("u2_turned"), 1)
            pe.wait_ge(sem("u2T_ready"), 6)
            for c in range(TC):
                for k in range(KD):
                    pe.matmul(ps[:, 6, c * NE:(c + 1) * NE], u2T[:, k, c * P:(c + 1) * P], wr[:, k, :], start=(k == 0), stop=False)
                last = pe.matmul(ps[:, 6, c * NE:(c + 1) * NE], ones[0:1, :], brow[0:1, :], start=False, stop=True)
            last.then_inc(sem("lg_done"), 1)
            pe.wait_ge(sem("mask_ready"), 1)
            for c in range(TC):
                pe.matmul(ps[:, 7, c * NE:(c + 1) * NE], tri, mk[:, c, :], start=True, stop=(c == 0))
                for b in range(c):
                    pe.matmul(ps[:, 7, c * NE:(c + 1) * NE], ones[:, :], mk[:, b, :], start=False, stop=(b == c - 1))
            for c in range(TC):
                last = pe.matmul(ps[:, 7, TC * NE:(TC + 1) * NE], ones[:, :], mk[:, c, :], start=(c == 0), stop=(c == TC - 1))
            last.then_inc(sem("rank_done"), 1)
            pe.wait_ge(sem("gates_ready"), 1)
            for c in range(TC):
                last = pe.transpose(ps[0:NE, 0, c * P:(c + 1) * P], em[:, c, :], ident[:, :])
            last.then_inc(sem("gd_turned"), 1)
            pe.wait_ge(sem("gd_ready"), 1)
            for u in range(6):
                c, n = divmod(u, 2)
                pe.matmul(ps[:, u, :], GTd[:, c * P:(c + 1) * P], bdn[:, n * 512:(n + 1) * 512], start=True, stop=True).then_inc(sem("bd_done"), 1)
            pe.wait_ge(sem("ulo_ready"), TC)
            pe.wait_ge(sem("selz_edges"), 2)

            def gather(n):
                pe.wait_ge(sem("sel_ready"), n + 1)
                for w in range(2):
                    cols = slice(w * 512, (w + 1) * 512)
                    for c in range(TC):
                        pe.matmul(ps[:, 6 + w, :], selz[:, c, S:3 * S], uhi[:, c, cols], start=(c == 0), stop=False)
                        last = pe.matmul(ps[:, 6 + w, :], selz[:, c, 0:2 * S], ulo[:, c, cols], start=False, stop=(c == TC - 1))
                last.then_inc(sem("gathered"), 1)

            def turn_rows(n):
                pe.wait_ge(sem("xr_ready"), n + 1)
                for k in range(KD):
                    last = pe.transpose(ps[:, 6 + k // 4, (k % 4) * P:(k % 4 + 1) * P], yS[:, k * P:(k + 1) * P], ident[:, :])
                last.then_inc(sem("x_turned"), 1)

            pe.wait_ge(sem("pos_ready"), 1)
            gather(0)
            turn_rows(0)

            def body(i, ahead=True, between=True):
                do_i, do_j, do_m = lags(i, ahead, between)

                def products(p, n, pairs):
                    for q in range(2):
                        if p in NATIVE:
                            if q == 0:
                                pe.wait_ge(sem(f"piece_in{p}"), 16 * n + 16)
                        else:
                            pe.wait_ge(sem("lo_made"), order(p, n, ahead, q))
                        for dst, x2, col, first, final in pairs[q]:
                            cols = slice(col, col + 512)
                            if p in NATIVE:
                                last = pe.matmul(dst, x2.bitcast(fp32), raw[:, p, q * 1024 + col:q * 1024 + col + 512], start=first, stop=final)
                            else:
                                pe.matmul(dst, x2, ringhi[:, ring_slot[p, q], cols], start=first, stop=False)
                                last = pe.matmul(dst, x2, ringlo[:, ring_slot[p, q], cols], start=False, stop=final)
                        if p not in NATIVE:
                            last.then_inc(sem("split_used"), 1)
                        elif q == 1:
                            last.then_inc(sem(f"native_used{p}"), 1)

                def gu(p):
                    products(p, i, [[(ps[:, n, :], xT[:, p, :], (n % 2) * 512, p == 0, p == 7) for n in (2 * q, 2 * q + 1)] for q in range(2)])

                def dn(p):
                    products(p, i - 1, [[(ps[:, 4 + n, :], actT[:, 2 * (p - 8) + q, :], n * 512, p == 8 and q == 0, p == 11 and q == 1)
                                         for n in range(2)] for q in range(2)])

                def scatter(us):
                    for u in us:
                        c, n = divmod(u, 2)
                        if u >= 2:
                            pe.wait_ge(sem("added"), 6 * (i - 1) + u - 1)
                        else:
                            pe.wait_ge(sem("gt_ready"), i - 1)
                            pe.wait_ge(sem("yS_ready"), i - 1)
                            if do_j and not do_i:
                                pe.wait_ge(sem("biased"), 2 * i)
                        pe.matmul(ps[:, 6 + n, :], GT[:, c * P:(c + 1) * P], yS[:, n * 512:(n + 1) * 512], start=True, stop=True).then_inc(sem("scattered"), 1)

                def turn_gates():
                    pe.wait_ge(sem("gm_ready"), i - 1)
                    pe.wait_ge(sem("biased"), 2 * (i if do_i else i - 1))
                    for c in range(TC):
                        last = pe.transpose(ps[:, 6 if do_i else 0, c * P:(c + 1) * P], Gm[:, c, :], ident[:, :])
                    last.then_inc(sem("gt_turned"), 1)

                if do_i:
                    pe.wait_ge(sem("xT_ready"), i + 1)
                    if do_j:
                        pe.wait_ge(sem("guS_ready"), 2 * i)
                    else:
                        pe.wait_ge(sem("added"), 6)
                    gu(0)
                elif do_j:
                    pe.wait_ge(sem("guS_ready"), 2 * i)
                    turn_gates()
                if do_j:
                    for f in range(NF):
                        last = pe.transpose(ps[:, 6 + f // 8, (f % 8) * S:(f % 8 + 1) * S], guS[:, f * P:(f + 1) * P], ident[0:S, 0:S])
                    last.then_inc(sem("gu_turned"), 1)
                if do_i:
                    gu(1)
                if do_m and (do_i or not do_j):
                    turn_gates()
                if do_i:
                    gu(2)
                if do_m:
                    scatter((0, 1))
                if do_i:
                    gu(3)
                if do_m:
                    scatter((2, 3))
                if do_i:
                    gu(4)
                if do_m:
                    scatter((4, 5))
                if do_i:
                    gu(5)
                    gu(6)
                    if do_m:
                        pe.wait_ge(sem("added"), 6 * i)
                    elif do_j:
                        pe.wait_ge(sem("biased"), 2 * i)
                    gather(i + 1)
                    gu(7)
                if do_j:
                    pe.wait_ge(sem("act_lo"), i)
                    if do_m:
                        pe.wait_ge(sem("yS_ready"), i - 1)
                    dn(8)
                if do_i:
                    turn_rows(i + 1)
                if do_j:
                    for p in (9, 10, 11):
                        dn(p)

            passes(pe, body)


_INS = ["x_prompt", "x_sample", "state_conv", "state_lru", "state_gla", "meta", "g_mix", "w_in", "conv_w", "conv_b",
        "w_rg_a", "b_rg_a", "w_rg_x", "b_rg_x", "lam", "gn_a", "w_gate_up", "b_gate", "gn_b", "w_out", "g_ffn",
        "w_router", "b_router", "w_gu", "b_gu", "w_down", "b_down", "g_final"]
_OUTS = [("y_p", (1, 256, 1024)), ("y_s", (8, 1, 1024)), ("conv_p", (1, 1, 3, 512)), ("lru_p", (1, 1, 512)),
         ("gla_p", (1, 1, 4, 64, 128)), ("conv_s", (1, 8, 3, 512)), ("lru_s", (1, 8, 512)), ("gla_s", (1, 8, 4, 64, 128))]


def kernel(**inputs):
    import numpy as np
    import concourse.bacc as bacc
    from concourse.bass_utils import run_bass_kernel_spmd

    nc = bacc.Bacc("TRN2", target_bir_lowering=False, num_devices=1)
    arrays, ins, outs = {}, {}, {}
    for name in _INS:
        a = np.ascontiguousarray(inputs[name])
        arrays[f"in_{name}"] = a
        ins[name] = nc.dram_tensor(f"in_{name}", a.shape, mybir.dt.from_np(a.dtype), kind="ExternalInput").ap()
    for name, shape in _OUTS:
        outs[name] = nc.dram_tensor(f"out_{name}", shape, mybir.dt.float32, kind="ExternalOutput").ap()
    hybrid_layer_kernel(nc, ins, outs)
    r = run_bass_kernel_spmd(nc, [arrays], core_ids=[0])
    return tuple(r.results[0][f"out_{name}"] for name, _ in _OUTS)
```

```python
import concourse.bass as bass
from concourse import mybir
from contextlib import ExitStack


def hybrid_layer_kernel(nc, A, O):
    fp32 = mybir.dt.float32
    f32r = mybir.dt.float32r
    i32 = mybir.dt.int32
    ALU = mybir.AluOpType
    ACT = mybir.ActivationFunctionType
    AX = mybir.AxisListType

    P = 128
    NM = A["meta"].shape[0]
    SEQ, D = A["x_prompt"].shape[1:]
    NB = A["x_sample"].shape[0]
    TP = NM + SEQ
    NT = TP + NB
    DA = A["state_lru"].shape[2]
    HB, DK, DV = A["state_gla"].shape[2:]
    GR = A["w_gate_up"].shape[1]
    NE, FF = A["w_gu"].shape[1], A["w_down"].shape[2]
    EPS = 1e-6
    CH = 64
    SB = 16
    NCH = SEQ // CH
    NSB = CH // SB
    KD = D // P
    MA = DA // P
    HP = HB // 2
    TC = 3
    TL = NT - 2 * P
    NF = 2 * FF // P
    C_RG, TAU, TOPK = 8.0, 16.0, 4
    ALPHA, LIMIT = 1.702, 7.0
    CLAMP = 40.0
    S = 64
    NV = NE * -(-NT // S)

    NPIECE = 12
    NATIVE = (2, 9)
    GU = list(range(8))
    DN = list(range(8, 12))
    split_gu = [p for p in GU if p not in NATIVE]
    split_dn = [p for p in DN if p not in NATIVE]
    ring_slot = {(p, q): 2 * (n % 2) + q for n, p in enumerate(split_gu + split_dn) for q in range(2)}
    assert len(split_gu + split_dn) % 2 == 0
    TURNS = len(split_gu) % 2 == 1

    def order(p, n, ahead=True, q=1):
        ng, nd = 2 * len(split_gu), 2 * len(split_dn)
        if p in GU:
            before = 0 if isinstance(n, int) and n == 0 else n * (ng + nd) - nd
            return before + 2 * split_gu.index(p) + q + 1
        return (n + 1) * (ng + nd) - nd + (ng if ahead else 0) + 2 * split_dn.index(p) + q + 1

    BY_POOL = [(3, 0), (4, 1), (6, 0), (8, 1), (11, 1)]

    def low_order(p, n, ahead=True, q=1):
        mine = (p, q) in BY_POOL
        gu, dn = ([(a, b) for a in pieces for b in range(2) if ((a, b) in BY_POOL) == mine] for pieces in (split_gu, split_dn))
        if p in GU:
            before = 0 if isinstance(n, int) and n == 0 else n * (len(gu) + len(dn)) - len(dn)
            at = before + gu.index((p, q)) + 1
        else:
            at = (n + 1) * (len(gu) + len(dn)) - len(dn) + (len(gu) if ahead else 0) + dn.index((p, q)) + 1
        return "lo_made_pool" if mine else "lo_made", at

    ctx = ExitStack()
    with ctx:
        sems = {}

        def sem(name):
            if name not in sems:
                sems[name] = ctx.enter_context(nc.semaphore(name))
            return sems[name]

        def sb(stack, name, shape, dt=fp32):
            return stack.enter_context(nc.sbuf_tensor(name, shape, dt))

        raw = sb(ctx, "raw", [P, NPIECE, 2048])
        yacc = sb(ctx, "yacc", [P, TC, D])
        ident = sb(ctx, "ident", [P, P])
        slot_no = sb(ctx, "slot_no", [P, 2 * S])
        ones = sb(ctx, "ones", [P, P])
        pv = sb(ctx, "pv", [P, 47])
        bguT = sb(ctx, "bguT", [P, NF, NE])
        pos = sb(ctx, "pos", [P, TC, NV + 2])
        gate = sb(ctx, "gate", [P, TC, NE])
        small = sb(ctx, "small", [P, 112])
        flag = sb(ctx, "flag", [P, 1], i32)
        G_MIX, CONV_W, CONV_B, BRA, BRX, LAM, GNA, BGATE, GNB = 0, 8, 24, 28, 32, 36, 40, 44, 46

        mx = ExitStack()
        wv = sb(mx, "wv", [P, 3, KD, 512])
        uT = sb(mx, "uT", [P, KD, NT])
        proj = sb(mx, "proj", [P, 20, NT])
        wlr = sb(mx, "wlr", [P, KD, GR])
        gup = sb(mx, "gup", [GR, HB * DK])
        lrT = sb(mx, "lrT", [GR, NT])
        seg = sb(mx, "seg", [P, NT])
        cm = sb(mx, "cm", [CH, CH])
        spare = sb(mx, "spare", [P, 2, MA, NT])
        mx.close()

        me = ExitStack()
        uhi = sb(me, "uhi", [P, TC, D], f32r)
        ulo = sb(me, "ulo", [P, TC, D], f32r)
        ringhi = sb(me, "ringhi", [P, 4, 1024], f32r)
        ringlo = sb(me, "ringlo", [P, 4, 1024], f32r)
        xT = sb(me, "xT", [P, KD, 2 * S], f32r)
        actT = sb(me, "actT", [P, KD, 2 * S], f32r)
        selz = sb(me, "selz", [P, TC, 3 * S], f32r)
        xr = sb(me, "xr", [P, D])
        Gm = sb(me, "Gm", [P, TC, 2 * S])
        GT = sb(me, "GT", [P, TC * P], f32r)
        guS = sb(me, "guS", [S, 2048])
        yhi = sb(me, "yhi", [P, D], f32r)
        ylo = sb(me, "ylo", [P, D], f32r)
        hS = sb(me, "hS", [P, 2, 8 * S])
        me.close()
        ps = ctx.enter_context(nc.psum_tensor("ps", [P, 8, 512], fp32))

        def flat(a):
            return a.rearrange("p a n -> p (a n)")

        wqk = flat(raw[:, 8:10, :]).rearrange("p (k n) -> p k n", n=512)
        wxa = flat(raw[:, 10:12, :]).rearrange("p (k n) -> p k n", n=512)
        wout = wv[:, 1:3].rearrange("p a k n -> p (a k n)").rearrange("p (k n) -> p k n", n=D)

        class Area:

            def __init__(self, ap):
                self.ap, self.at = ap, 0

            def cut(self, *dims):
                n = 1
                for d in dims:
                    n *= d
                got = self.ap[:, self.at:self.at + n]
                self.at += n
                assert self.at <= self.ap.shape[1]
                if len(dims) == 2:
                    got = got.rearrange("p (a b) -> p a b", a=dims[0])
                elif len(dims) == 3:
                    got = got.rearrange("p (a b c) -> p a b c", a=dims[0], b=dims[1])
                return got

        early = Area(flat(raw[:, 4:8, :]))
        cs = early.cut(MA, 32)
        la = early.cut(HP, NT)
        bc = early.cut(HP, NT)
        ta = early.cut(HP, NT)
        qI = early.cut(HP, NT)
        qE = early.cut(HP, NT)
        kD = early.cut(HP, TP)
        kI = early.cut(HP, NSB, SEQ)
        kIl = early.cut(HP, NM)
        PT = early.cut(NCH + 1, HB, CH)
        XW = TP + 3
        xp = early.cut(MA, XW)
        assert early.at <= 4 * 2048
        first = Area(flat(raw[:, 4:8, :]))
        first.cut(MA, 32)
        xn = first.cut(TC, D)
        pin = first.cut(P)
        cst = first.cut(DA)
        bgr = first.cut(2 * FF)
        Sg = [flat(la)[:, n * HP * DV:(n + 1) * HP * DV].rearrange("p (a v) -> p a v", a=HP) for n in range(2)]
        second = Area(flat(raw[:, 8:10, :]))
        VT = second.cut(NCH + 1, HB * DV)
        KT = second.cut(NCH + 1, HB * DK)
        third = Area(flat(raw[:, 10:12, :]))
        xc = third.cut(MA, NT)
        rr = third.cut(MA, NT)
        ii = third.cut(MA, NT)
        vs = third.cut(HB * DV)
        aa, tt = spare[:, 0], spare[:, 1]
        S0 = flat(wv[:, 0])[:, 0:2048].rearrange("p (b a v) -> p b a v", b=NB, a=HP)
        Sn = flat(wv[:, 0])[:, 2048:4096].rearrange("p (b a v) -> p b a v", b=NB, a=HP)
        kflat = kI.rearrange("p a b n -> p (a b n)")
        T2 = kflat[:, 0:MA * NT].rearrange("p (m n) -> p m n", m=MA)
        NO = 3 + NB + 1 + NB
        OT = kflat[:, 1120:1120 + MA * NO].rearrange("p (m n) -> p m n", m=MA)
        OS = kflat[0:NO, 1280:1280 + DA]
        T3 = early.ap[:, 1808:1808 + MA * NT].rearrange("p (m n) -> p m n", m=MA)
        eS = small[:, 24:24 + HP * NB].rearrange("p (a b) -> p a b", a=HP)
        qS_AT = (40, 93)
        qS = [small[:, n:n + HP * NB].rearrange("p (a b) -> p a b", a=HP) for n in qS_AT]
        qE = [qE, ta]
        eb = small[:, 56:56 + HP * (NCH + 1)].rearrange("p (a c) -> p a c", a=HP)
        eps = small[:, 110:111]
        slot_gate = small[:, 109:110]
        ssq, rstd = small[:, 0:3], small[:, 4:7]
        nsp8, la0, la1, la2 = (small[:, 8 + 4 * n:12 + 4 * n] for n in range(4))
        WA = flat(tt)[:, 0:MA * P].rearrange("p (m n) -> p m n", m=MA)
        WX = flat(tt)[:, MA * P:2 * MA * P].rearrange("p (m n) -> p m n", m=MA)
        u2 = flat(raw[:, 8:10, :])[:, 0:TC * D].rearrange("p (c d) -> p c d", c=TC)
        rt = Area(flat(raw[:, 8:10, :]))
        rt.cut(TC * D)
        wr = rt.cut(KD, NE)
        brow = rt.cut(NE)
        lg = rt.cut(TC, NE)
        em = rt.cut(TC, NE)
        mk = rt.cut(TC, NE)
        eq = rt.cut(TC, NE)
        gtv = rt.cut(TC, NE)
        u2T = flat(raw[:, 10:12, :])[:, 0:KD * TC * P].rearrange("p (k t) -> p k t", k=KD)
        gff = flat(raw[:, 10:12, :])[:, 3072:4096]
        tri = xr[:, 0:P]
        valid = small[:, 90:93]
        bdn = flat(hS)[0:NE, :]
        GTd = guS[0:NE, 0:TC * P]
        gfin = flat(raw[:, 0:1, :])[:, 0:D]
        yout = flat(raw[:, 1:3, :])[:, 0:TC * D].rearrange("p (c d) -> p c d", c=TC)
        junk = raw[:, 4, 0:D]

        chunks = [(0, NM)] + [(NM + CH * c, CH) for c in range(NCH)]
        rows_of = [P, P, TL]
        sampled = ps[:, 7, 0:2 * HP * NB].rearrange("p (a b h) -> p a h b", a=HP, h=2)


        x = A["x_prompt"]
        block = ctx.enter_context(nc.Block())

        TILES = [("in_lr", lambda k: wlr[:, k, :], None)]
        for name, w, slot in (("in_qk", wqk, 0), ("in_xa", wxa, 8), ("in_v", wv[:, 0], 4), ("in_ya", wv[:, 1], 12), ("in_g", wv[:, 2], 16)):
            for m in range(4):
                TILES.append((name, (lambda k, w=w, m=m: w[:, k, m * P:(m + 1) * P]), slot + m))
        XA_TILES, V_TILES, YA_TILES, G_TILES = (range(4 * n + 5, 4 * n + 9) for n in range(4))
        BY_DVE = 5

        def evacuator(t):
            return ("proj_dve", t + 1) if t < BY_DVE else ("proj_act", t + 1 - BY_DVE)

        def e_of(i):
            return i if isinstance(i, int) else i % NE

        def by_tile(ap):
            return ap.rearrange("a (r c) -> (a r) c", c=P)

        by_act = [(pin[0:8, :], by_tile(A["g_mix"])), (pin[8:24, :], by_tile(A["conv_w"][0])),
                  (cst[0:24, :], A["state_conv"][0].rearrange("b j n -> (b j) n")), (cst[24:32, :], A["state_lru"][0]),
                  (bgr[0:NE, :], A["b_gu"][0]), (pin[36:40, :], by_tile(A["lam"])), (pin[40:44, :], by_tile(A["gn_a"]))]
        by_pool = [(pin[24:28, :], by_tile(A["conv_b"])), (pin[28:32, :], by_tile(A["b_rg_a"])), (pin[32:36, :], by_tile(A["b_rg_x"])),
                   (pin[44:46, :], by_tile(A["b_gate"])), (pin[46:47, :], A["gn_b"])]

        @block.sync
        def _(sp):
            def load(dst, src, name):
                sp.dma_start(dst, src).then_inc(sem(name), 16)

            load(yacc[0:NM, 0, :], A["meta"], "x_in")
            load(yacc[NM:P, 0, :], x[0, 0:P - NM, :], "x_in")
            load(yacc[:, 1, :], x[0, P - NM:2 * P - NM, :], "x_in")
            sp.wait_ge(sem("tail_zero"), 1)
            load(yacc[0:TP - 2 * P, 2, :], x[0, 2 * P - NM:SEQ, :], "x_in")
            load(yacc[TP - 2 * P:TL, 2, :], A["x_sample"][:, 0, :], "x_in")
            win = A["w_in"][0].rearrange("(k p) n -> p k n", p=P)
            load(wlr[:, :, :], win[:, :, 2560:2576], "in_lr")
            sp.wait_ge(sem("par_in"), 16 * len(by_act))
            sp.wait_ge(sem("par_in_pool"), 16 * len(by_pool))
            load(wqk, win[:, :, 2 * DA:2 * DA + 512], "in_qk")
            load(gup[:, :], A["w_gate_up"][0], "gup_in")
            load(wxa, win[:, :, 0:512], "in_xa")
            load(wv[:, 0], win[:, :, 1536:2048], "in_v")
            load(wv[:, 1], win[:, :, 512:1024], "in_ya")
            load(wv[:, 2], win[:, :, 2048:2560], "in_g")
            for p in range(4):
                load(raw[:, p, :], A["w_gu"][0, 0, p * P:(p + 1) * P, :], f"piece_in{p}")
            sp.wait_ge(sem("proj_done"), V_TILES[-1] + 1)
            for b in range(NB):
                load(S0[:, b], A["state_gla"][0, b].rearrange("(a h) k v -> (h k) a v", h=2), "s0_in")
            sp.wait_ge(sem("proj_done"), len(TILES))
            load(wout, A["w_out"][0].rearrange("(k p) n -> p k n", p=P), "wout_in")
            sp.wait_ge(sem("gla_state"), NCH + 1)
            sp.dma_start(O["gla_p"][0, 0].rearrange("(a h) k v -> (h k) a v", h=2), Sg[NCH % 2]).then_inc(sem("out_mix"), 16)
            sp.wait_ge(sem("sample_state"), 1)
            for b in range(NB):
                sp.dma_start(O["gla_s"][0, b].rearrange("(a h) k v -> (h k) a v", h=2), Sn[:, b]).then_inc(sem("out_mix"), 16)
            sp.wait_ge(sem("rows_ready"), 1)
            sp.dma_start(O["conv_p"][0, 0], OS[0:3, :]).then_inc(sem("out_mix"), 16)
            sp.dma_start(O["conv_s"][0, :, 0:2, :], A["state_conv"][0, :, 1:3, :]).then_inc(sem("out_mix"), 16)
            sp.dma_start(O["conv_s"][0, :, 2, :], OS[3:3 + NB, :]).then_inc(sem("out_mix"), 16)
            sp.dma_start(O["lru_p"][0], OS[3 + NB:4 + NB, :]).then_inc(sem("out_mix"), 16)
            sp.dma_start(O["lru_s"][0], OS[4 + NB:NO, :]).then_inc(sem("out_mix"), 16)
            sp.wait_ge(sem("out_mix"), 16 * (1 + NB + 5))
            sp.wait_ge(sem("mix_ready"), MA + 1)
            load(gff, A["g_ffn"].broadcast_to([P, D]), "router_in")
            load(wr, A["w_router"][0].rearrange("(k p) e -> p k e", p=P), "router_in")
            load(brow[0:1, :], A["b_router"], "router_in")
            sp.wait_ge(sem("h_ready"), 6)
            load(bdn, A["b_down"][0], "bdn_in")

            def piece(p, i, first=False):
                if not first:
                    if p in NATIVE:
                        sp.wait_ge(sem(f"native_used{p}"), i)
                    else:
                        sp.wait_ge(sem("split_used"), order(p, i - 1))
                e = e_of(i)
                if p in GU:
                    src = A["w_gu"][0, bass.ds(e, 1), p * P:(p + 1) * P, :].rearrange("e p n -> (e p) n")
                    load(raw[:, p, :], src, f"piece_in{p}")
                else:
                    r = (p - 8) * 2 * P
                    src = A["w_down"][0, bass.ds(e, 1), r:r + 2 * P, :].rearrange("e (k p) n -> p (e k) n", p=P)
                    load(raw[:, p, :].rearrange("p (k n) -> p k n", k=2), src, f"piece_in{p}")

            for p in range(4, 8):
                piece(p, 0, first=True)
            sp.wait_ge(sem("gd_turned"), 1)
            sp.wait_ge(sem("pos_ready"), 1)
            for p in DN:
                piece(p, 0, first=True)
            for p in GU:
                piece(p, 1)
            with sp.Fori(2, NE) as i:
                for p in GU:
                    piece(p, i)
                for p in DN:
                    piece(p, i - 1)
            sp.wait_ge(sem("flag_ready"), 1)
            over = sp.value_load(flag[0:1, 0:1], min_val=0, max_val=1)
            last = over * (NV - NE) + NE
            with sp.If(over):
                with sp.Fori(NE, NV) as i:
                    for p in GU:
                        piece(p, i)
                    for p in DN:
                        piece(p, i - 1)
            for p in DN:
                if p in NATIVE:
                    sp.wait_ge(sem(f"native_used{p}"), last - 1)
                else:
                    sp.wait_ge(sem("split_used"), order(p, last - 2))
                r = (p - 8) * 2 * P
                load(raw[:, p, :].rearrange("p (k n) -> p k n", k=2),
                     A["w_down"][0, NE - 1, r:r + 2 * P, :].rearrange("(k p) n -> p k n", p=P), f"piece_in{p}")
            sp.wait_ge(sem("split_used"), order(7, last - 1))
            load(gfin, A["g_final"].rearrange("(a n) -> a n", a=1).broadcast_to([P, D]), "gfin_in")
            sp.wait_ge(sem("y_ready"), 1)
            sp.dma_start(O["y_p"][0, 0:P - NM, :], yout[NM:P, 0, :]).then_inc(sem("out_y"), 16)
            sp.wait_ge(sem("y_ready"), 2)
            sp.dma_start(O["y_p"][0, P - NM:2 * P - NM, :], yout[:, 1, :]).then_inc(sem("out_y"), 16)
            sp.wait_ge(sem("y_ready"), 3)
            sp.dma_start(O["y_p"][0, 2 * P - NM:SEQ, :], yout[0:TP - 2 * P, 2, :]).then_inc(sem("out_y"), 16)
            sp.dma_start(O["y_s"][:, 0, :], yout[TP - 2 * P:TL, 2, :]).then_inc(sem("out_y"), 16)
            sp.wait_ge(sem("out_y"), 64)

        def passes(eng, body):
            body(0)
            body(1)
            with eng.Fori(2, NE) as i:
                body(i)
            eng.wait_ge(sem("flag_ready"), 1)
            over = eng.value_load(flag[0:1, 0:1], min_val=0, max_val=1)
            with eng.If(over):
                with eng.Fori(NE, NV) as i:
                    body(i)
            last = over * (NV - NE) + NE
            body(last, ahead=False)
            body(last + 1, ahead=False, between=False)
            return last

        EARLY = [(0, 0), (1, 0), (0, 1), (1, 1)]

        def early(p, n):
            return isinstance(n, int) and (p, n) in EARLY

        def lags(i, ahead, between):
            n = i if isinstance(i, int) else NE
            return ahead, between and n >= 1, n >= 2

        def ring_free(eng, p, n, ahead, q):
            turn = (p == split_gu[0] and isinstance(n, int) and n == 1) or (p == split_dn[0] and not ahead)
            at = order(p, n, ahead, q) - (2 if turn and TURNS else 4)
            if not isinstance(at, int) or at > 0:
                eng.wait_ge(sem("split_used"), at)

        def lower(eng, p, n, ahead, q):
            eng.wait_ge(sem("hi_made"), order(p, n, ahead, q))
            ring_free(eng, p, n, ahead, q)
            eng.tensor_tensor(ringlo[:, ring_slot[p, q], :], raw[:, p, q * 1024:(q + 1) * 1024],
                              ringhi[:, ring_slot[p, q], :].bitcast(fp32), ALU.subtract).then_inc(sem(low_order(p, n, ahead, q)[0]), 1)

        @block.gpsimd
        def _(pool):
            for dst, src in by_pool:
                pool.dma_start(dst, src).then_inc(sem("par_in_pool"), 16)
            pool.memset(ident[:, :], 0.0).then_inc(sem("zeroed"), 1)
            pool.memset(ones[:, :], 1.0).then_inc(sem("zeroed"), 1)
            pool.memset(cm[:, :], 1.0).then_inc(sem("zeroed"), 1)
            pool.memset(WA, 0.0).then_inc(sem("zeroed"), 1)
            pool.memset(WX, 0.0).then_inc(sem("zeroed"), 1)
            pool.wait_ge(sem("zeroed"), 5)
            pool.affine_select(out=ident[:, :], in_=ident[:, :], compare_op=ALU.not_equal, fill=1.0,
                               base=0, pattern=[[-1, P]], channel_multiplier=1).then_inc(sem("ident_ready"), 1)
            pool.affine_select(out=cm[:, :], in_=cm[:, :], compare_op=ALU.is_ge, fill=0.0,
                               base=0, pattern=[[1, CH]], channel_multiplier=-1).then_inc(sem("cm_ready"), 1)
            pool.iota(slot_no[:, :].rearrange("p (a s) -> p a s", a=2), pattern=[[0, 2], [1, S]], base=0,
                      channel_multiplier=0, allow_small_or_imprecise_dtypes=True).then_inc(sem("slot_no_ready"), 1)
            for m in range(MA):
                for h in range(2):
                    r = slice(64 * h, 64 * h + 64)
                    pool.dma_start(WA[r, m, 64 * h:64 * h + 64], A["w_rg_a"][0, 2 * m + h]).then_inc(sem("wrg_in"), 16)
                    pool.dma_start(WX[r, m, 64 * h:64 * h + 64], A["w_rg_x"][0, 2 * m + h]).then_inc(sem("wrg_in"), 16)
            pool.wait_ge(sem("h_ready"), 6)
            pool.memset(tri, 1.0).then_inc(sem("pool_own"), 1)
            pool.memset(valid, 1.0).then_inc(sem("pool_own"), 1)
            pool.wait_ge(sem("pool_own"), 2)
            pool.affine_select(out=tri, in_=tri, compare_op=ALU.is_ge, fill=0.0, base=-1,
                               pattern=[[1, P]], channel_multiplier=-1).then_inc(sem("tri_ready"), 1)
            pool.affine_select(out=valid, in_=valid, compare_op=ALU.is_ge, fill=0.0, base=NT - 1,
                               pattern=[[-P, TC]], channel_multiplier=-1).then_inc(sem("tri_ready"), 1)

            def body(i, ahead=True, between=True):
                do_i, do_j, _ = lags(i, ahead, between)
                for p in GU:
                    if do_i:
                        for q in range(2):
                            if (p, q) in BY_POOL:
                                lower(pool, p, i, ahead, q)
                    if p == 3 and do_j:
                        pool.wait_ge(sem("gm_hot"), i)
                        pool.tensor_tensor(Gm[:, :, :], Gm[:, :, :], gate[:, :, bass.ds(e_of(i - 1), 1)].broadcast_to([P, TC, 2 * S]),
                                           ALU.mult).then_inc(sem("gm_ready"), 1)
                for p in DN:
                    for q in range(2):
                        if do_j and (p, q) in BY_POOL:
                            lower(pool, p, i - 1, ahead, q)

            pool.wait_ge(sem("pos_ready"), 1)
            passes(pool, body)

        @block.scalar
        def _(act):
            chain = [0]

            def link(ins):
                chain[0] += 1
                ins.then_inc(sem("act_chain"), 1)
                act.wait_ge(sem("act_chain"), chain[0])

            for dst, src in by_act:
                act.dma_start(dst, src).then_inc(sem("par_in"), 16)
            act.wait_ge(sem("x_in"), 80)
            for c in range(TC):
                act.activation(xn[:, c, :], yacc[:, c, :], ACT.Square, accum_out=ssq[:, c:c + 1]).then_inc(sem("ssq"), 1)
            act.wait_ge(sem("var"), 1)
            act.activation(rstd, ssq, ACT.Sqrt).then_inc(sem("std"), 1)
            act.wait_ge(sem("lam_abs"), 1)
            act.activation(la1, la0, ACT.Exp, scale=-1.0).then_inc(sem("lam_exp"), 1)
            act.wait_ge(sem("z_abs"), 1)
            link(act.activation(bc, bc, ACT.Exp, scale=-1.0))
            act.activation(bc, bc, ACT.Ln, bias=1.0).then_inc(sem("z_log"), 1)
            act.wait_ge(sem("shifted"), 1)
            act.activation(eb, bc[:, :, NM - 1:TP:CH], ACT.Exp).then_inc(sem("decays"), 1)
            act.activation(eS, bc[:, :, TP:NT], ACT.Exp).then_inc(sem("decays"), 1)
            act.activation(qE[0], bc, ACT.Exp).then_inc(sem("decays"), 1)
            act.activation(qI[:, :, 0:TP], ta[:, :, 0:TP], ACT.Exp).then_inc(sem("decays"), 1)
            act.wait_ge(sem("shifted"), 2)
            act.activation(kI.rearrange("p a b n -> p (a b n)"), kI.rearrange("p a b n -> p (a b n)"), ACT.Exp).then_inc(sem("decays"), 1)
            act.activation(kIl, kIl, ACT.Exp).then_inc(sem("decays"), 1)
            act.activation(kD, kD, ACT.Exp).then_inc(sem("decays"), 1)
            def take(t, function):
                act.wait_ge(sem("proj_done"), t + 1)
                act.activation(proj[:, TILES[t][2], :], ps[:, t % 4, 0:NT], function).then_inc(sem("proj_act"), 1)

            for t in (*XA_TILES, *V_TILES):
                take(t, ACT.Copy)
            for c, (t0, n) in enumerate(chunks):
                act.wait_ge(sem("turned"), c + 1)
                act.activation(VT[0:n, c, :], ps[0:n, 4 + 2 * (c % 2), :], ACT.Copy).then_inc(sem("vt"), 1)
                act.activation(KT[0:n, c, :], ps[0:n, 5 + 2 * (c % 2), 0:HB * DK], ACT.Copy).then_inc(sem("vt"), 1)
            act.wait_ge(sem("vs_turned"), 1)
            act.activation(vs[0:NB, :], ps[0:NB, 6, :], ACT.Copy).then_inc(sem("vs_ready"), 1)
            for t in YA_TILES:
                take(t, ACT.Gelu_apprx_tanh)
            for m in range(MA):
                act.wait_ge(sem("rg_done"), 2 * m + 1)
                act.activation(rr[:, m, :], ps[:, 4 + 2 * (m % 2), 0:NT], ACT.Sigmoid, bias=pv[:, BRA + m:BRA + m + 1]).then_inc(sem("rg_sig"), 1)
                act.wait_ge(sem("rg_done"), 2 * m + 2)
                act.activation(ii[:, m, :], ps[:, 5 + 2 * (m % 2), 0:NT], ACT.Sigmoid, bias=pv[:, BRX + m:BRX + m + 1]).then_inc(sem("rg_sig"), 1)
            act.wait_ge(sem("log_a"), 1)
            act.activation(aa, rr, ACT.Exp).then_inc(sem("a_ready"), 1)
            link(act.activation(tt, rr, ACT.Tanh, scale=-1.0))
            link(act.activation(T2, tt, ACT.Ln, bias=1.0))
            act.activation(T2, T2, ACT.Exp, scale=-0.5).then_inc(sem("a_ready"), 1)
            act.activation(tt, tt, ACT.Sqrt, scale=2.0).then_inc(sem("om_root"), 1)
            for t in G_TILES:
                take(t, ACT.Silu)
            act.wait_ge(sem("eps_ready"), 1)
            act.wait_ge(sem("a_sum"), 1)
            act.wait_ge(sem("b_used"), 1)
            link(act.activation(aa[:, 0, :], ps[:, 6, 0:NT], ACT.Ln, scale=1.0 / DA, bias=eps))
            act.activation(aa[:, 0, :], aa[:, 0, :], ACT.Exp, scale=-0.5).then_inc(sem("rstd_a"), 1)
            act.wait_ge(sem("o_done"), 1)
            act.wait_ge(sem("b_used"), 1)
            for a in range(HP):
                act.activation(tt[:, 2 * a:2 * a + 2, TP:NT], sampled[:, a], ACT.Square).then_inc(sem("o_sq"), 1)
            act.activation(tt[:, :, 0:TP], ps[:, 0:HB, 0:TP], ACT.Square).then_inc(sem("o_sq"), 1)
            act.wait_ge(sem("b_sum"), 1)
            link(act.activation(T3, ps[:, 4:8, 0:NT], ACT.Ln, scale=1.0 / DV, bias=eps))
            act.activation(T3, T3, ACT.Exp, scale=-0.5).then_inc(sem("rstd_b"), 1)

            def turn_u2(c):
                for n in (2 * c, 2 * c + 1):
                    act.wait_ge(sem("u2_turned"), n + 1)
                    act.activation(u2T[:, 4 * (n % 2):4 * (n % 2) + 4, c * P:(c + 1) * P],
                                   ps[:, n, :].rearrange("p (k t) -> p k t", k=4), ACT.Copy).then_inc(sem("u2T_ready"), 1)

            for c in range(TC):
                act.wait_ge(sem("h_ready"), 2 * c + 2)
                if c == 0:
                    act.wait_ge(sem("out_mix"), 16 * (1 + NB + 5))
                act.activation(u2[:, c, :], yacc[:, c, :], ACT.Square, accum_out=ssq[:, c:c + 1]).then_inc(sem("ssq"), 1)
                act.wait_ge(sem("var"), c + 2)
                act.activation(rstd[:, c:c + 1], ssq[:, c:c + 1], ACT.Sqrt).then_inc(sem("std"), 1)
                if c >= 1:
                    turn_u2(c - 1)
            for c in range(TC):
                act.wait_ge(sem("u2_ready"), c + 1)
                act.activation(uhi[:, c, :], u2[:, c, :], ACT.Copy).then_inc(sem("uhi_ready"), 1)
            turn_u2(TC - 1)

            def high_halves(p, n, ahead=True):
                if p not in NATIVE:
                    act.wait_ge(sem(f"piece_in{p}"), 16 * n + 16)
                    for q in range(2):
                        ring_free(act, p, n, ahead, q)
                        act.activation(ringhi[:, ring_slot[p, q], :], raw[:, p, q * 1024:(q + 1) * 1024], ACT.Copy).then_inc(sem("hi_made"), 1)

            for p, n in EARLY[:2]:
                high_halves(p, n)
            act.wait_ge(sem("lg_shift"), 1)
            act.activation(em, em, ACT.Exp).then_inc(sem("lg_exp"), 1)
            act.wait_ge(sem("gd_turned"), 1)
            act.activation(GTd, ps[0:NE, 0, 0:TC * P], ACT.Copy).then_inc(sem("gd_ready"), 1)

            def gathered_rows(n):
                act.wait_ge(sem("gathered"), n + 1)
                if not isinstance(n, int) or n >= 1:
                    act.wait_ge(sem("guS_ready"), 2 * n - 2)
                act.activation(xr[:, :].rearrange("p (a n) -> p a n", a=2), ps[:, 6:8, :], ACT.Copy).then_inc(sem("xr_ready"), 1)

            def turned_rows(n):
                act.wait_ge(sem("x_turned"), n + 1)
                if not isinstance(n, int) or n >= 1:
                    act.wait_ge(sem("split_used"), order(7, n - 1))
                act.activation(xT[:, :, :], ps[:, 6:8, :].rearrange("p a (k s) -> p (a k) s", k=4), ACT.Copy).then_inc(sem("xT_ready"), 1)

            gathered_rows(0)
            turned_rows(0)

            def body(i, ahead=True, between=True):
                do_i, do_j, do_m = lags(i, ahead, between)
                static = isinstance(i, int)

                def hi(p, n):
                    if not early(p, n):
                        high_halves(p, n, ahead)

                def low_rows(n):
                    if n == 0:
                        act.wait_ge(sem("split_used"), order(7, i))
                        act.wait_ge(sem("x_turned"), i + 2)
                    else:
                        act.wait_ge(sem("guS_ready"), 2 * i + 1)
                    act.activation(xr[0:S, :].rearrange("p (a n) -> p a n", a=2), ps[S:2 * S, 2 * n:2 * n + 2, :], ACT.Copy).then_inc(sem("low_ready"), 1)

                if do_i:
                    for p in (0, 1, 2, 3):
                        hi(p, i)
                if do_m:
                    act.wait_ge(sem("gt_turned"), i - 1)
                    turned = ps[:, 6 if do_i else 0, 0:TC * P]
                    act.activation(turned, turned, ACT.Copy, accum_out=slot_gate).then_inc(sem("slot_gate_ready"), 1)
                    act.wait_ge(sem("slot_gate_ready"), i - 1)
                    act.wait_ge(sem("split_used"), order(11, i - 2, do_j))
                    if not static or i >= 3:
                        act.wait_ge(sem("scattered"), 6 * (i - 2))
                    act.activation(yhi[:, :].rearrange("p (a n) -> p a n", a=2), ps[:, 4:6, :], ACT.Copy, scale=slot_gate).then_inc(sem("y_hi"), 1)
                if do_j and not do_i:
                    hi(8, i - 1)
                if do_j:
                    act.wait_ge(sem("clipped"), i)
                    act.wait_ge(sem("product"), i)
                    act.activation(hS[:, 0, :], hS[:, 0, :], ACT.Sigmoid, scale=ALPHA).then_inc(sem("sig_ready"), 1)
                if do_i:
                    hi(4, i)
                if do_j:
                    act.wait_ge(sem("acted"), i)
                    if not static or i >= 2:
                        act.wait_ge(sem("split_used"), order(11, i - 2))
                    act.activation(actT[:, :, 0:S], hS[:, 1, :].rearrange("p (k s) -> p k s", k=KD), ACT.Copy).then_inc(sem("act_hi"), 1)
                if do_i:
                    for p in (5, 6, 7):
                        hi(p, i)
                if do_i and do_j:
                    hi(8, i - 1)
                if do_i:
                    gathered_rows(i + 1)
                    if not do_j:
                        high_halves(*EARLY[2])
                if do_j:
                    hi(9, i - 1)
                    hi(10, i - 1)
                if do_i:
                    turned_rows(i + 1)
                    low_rows(0)
                if do_j:
                    hi(11, i - 1)
                elif do_i:
                    high_halves(*EARLY[3])
                if do_i:
                    low_rows(1)

            last = passes(act, body)
            for c in range(TC):
                act.wait_ge(sem("added"), 6 * last + 2 * c + 2)
                act.activation(junk, yacc[:, c, :], ACT.Square, accum_out=ssq[:, c:c + 1]).then_inc(sem("ssq"), 1)
                act.wait_ge(sem("ssq"), 2 * TC + c + 1)
            act.wait_ge(sem("var"), 2 + TC)
            act.activation(rstd, ssq, ACT.Sqrt).then_inc(sem("std"), 1)

        @block.vector
        def _(dve):
            chain = [0]

            def link(*many):
                for ins in many:
                    chain[0] += 1
                    ins.then_inc(sem("dve_chain"), 1)
                dve.wait_ge(sem("dve_chain"), chain[0])

            dve.memset(eps, EPS).then_inc(sem("eps_ready"), 1)
            dve.memset(yacc[:, 2, :], 0.0).then_inc(sem("tail_zero"), 1)
            link(dve.memset(seg[:, :], 1.0), dve.memset(xp[:, :, 0:3], 0.0))
            for t0, _ in chunks:
                dve.memset(seg[:, t0:t0 + 1], 0.0).then_inc(sem("seg_ready"), 1)
            dve.memset(seg[:, TP:NT], 0.0).then_inc(sem("seg_ready"), 1)
            dve.wait_ge(sem("par_turned"), 1)
            dve.tensor_copy(pv[:, :], ps[:, 0, 0:47]).then_inc(sem("par_ready"), 1)
            dve.tensor_copy(cs, ps[:, 1, 0:MA * 32].rearrange("p (m n) -> p m n", m=MA)).then_inc(sem("par_ready"), 1)
            dve.tensor_copy(bguT[:, :, :], ps[:, 2, :].rearrange("p (f e) -> p f e", f=NF)).then_inc(sem("par_ready"), 1)
            dve.wait_ge(sem("ssq"), TC)
            dve.tensor_scalar(ssq, ssq, 1.0 / D, EPS, ALU.mult, ALU.add).then_inc(sem("var"), 1)
            dve.wait_ge(sem("std"), 1)
            link(dve.reciprocal(rstd, rstd))
            for c in range(TC):
                dve.tensor_scalar(xn[:, c, :], yacc[:, c, :], rstd[:, c:c + 1], None, ALU.mult).then_inc(sem("xn_ready"), 1)
            dve.wait_ge(sem("par_ready"), 3)
            for k in range(KD):
                dve.wait_ge(sem("u_turned"), k + 1)
                dve.tensor_scalar(uT[:, k, :], ps[:, k, 0:NT], pv[:, G_MIX + k:G_MIX + k + 1], None, ALU.mult).then_inc(sem("uT_ready"), 1)
            lam = pv[:, LAM:LAM + MA]
            dve.scalar_tensor_tensor(out=la0, in0=lam, scalar=-1.0, in1=lam, op0=ALU.mult, op1=ALU.max).then_inc(sem("lam_abs"), 1)

            dve.wait_ge(sem("lam_exp"), 1)
            link(dve.tensor_scalar(la0, la1, 2.0, None, ALU.add))
            link(dve.reciprocal(la0, la0))
            link(dve.tensor_tensor(la0, la0, la1, ALU.mult))
            link(dve.tensor_tensor(la1, la0, la0, ALU.mult))
            link(dve.tensor_scalar(la2, la1, 1.0 / 19, 1.0 / 17, ALU.mult, ALU.add))
            for n in (15, 13, 11, 9, 7, 5, 3, 1):
                link(dve.tensor_tensor(la2, la2, la1, ALU.mult))
                link(dve.tensor_scalar(la2, la2, 1.0 / n, None, ALU.add))
            link(dve.tensor_tensor(la2, la2, la0, ALU.mult))
            link(dve.tensor_scalar(la1, lam, -1.0, 0.0, ALU.mult, ALU.max))
            link(dve.scalar_tensor_tensor(out=la2, in0=la2, scalar=2.0, in1=la1, op0=ALU.mult, op1=ALU.add))
            link(dve.tensor_scalar(nsp8, la2, -C_RG, None, ALU.mult))
            def take(t):
                dve.wait_ge(sem("proj_done"), t + 1)
                if t == 0:
                    dve.tensor_copy(lrT[:, :], ps[0:GR, 0, 0:NT]).then_inc(sem("proj_dve"), 1)
                else:
                    dve.tensor_copy(proj[:, TILES[t][2], :], ps[:, t % 4, 0:NT]).then_inc(sem("proj_dve"), 1)

            take(0)
            take(1)
            for a in range(HP):
                dve.wait_ge(sem("z_done"), a + 1)
                link(dve.tensor_scalar(la[:, a, :], ps[:, 4 + a, 0:NT], pv[:, BGATE + a:BGATE + a + 1], None, ALU.add))
            dve.scalar_tensor_tensor(out=bc, in0=la, scalar=-1.0, in1=la, op0=ALU.mult, op1=ALU.max).then_inc(sem("z_abs"), 1)
            link(dve.tensor_scalar(ta, la, 0.0, 1.0 / TAU, ALU.min, ALU.mult))
            dve.wait_ge(sem("z_log"), 1)
            link(dve.scalar_tensor_tensor(out=la, in0=bc, scalar=-1.0 / TAU, in1=ta, op0=ALU.mult, op1=ALU.add))
            dve.wait_ge(sem("seg_ready"), NCH + 2)
            link(*[dve.tensor_tensor_scan(out=bc[:, a, :], data0=seg[:, :], data1=la[:, a, :], initial=0.0,
                                          op0=ALU.mult, op1=ALU.add) for a in range(HP)])
            take(2)
            for a in range(HP):
                b16 = bc[:, a, 0:TP].rearrange("p (n s) -> p n s", s=SB)
                link(dve.tensor_tensor(ta[:, a, 0:TP].rearrange("p (n s) -> p n s", s=SB), b16,
                                       b16[:, :, SB // 2 - 1:SB // 2].broadcast_to([P, TP // SB, SB]), ALU.subtract))
            dve.tensor_scalar(ta[:, :, 0:TP], ta[:, :, 0:TP], CLAMP, None, ALU.min).then_inc(sem("shifted"), 1)
            take(3)
            for a in range(HP):
                b64 = bc[:, a, NM:TP].rearrange("p (c s) -> p c s", s=CH)
                for i in range(NSB):
                    mid = SB * i + SB // 2 - 1
                    link(dve.tensor_tensor(kI[:, a, i, :].rearrange("p (c s) -> p c s", s=CH),
                                           b64[:, :, mid:mid + 1].broadcast_to([P, NCH, CH]), b64, ALU.subtract))
                link(dve.tensor_tensor(kD[:, a, NM:TP].rearrange("p (c s) -> p c s", s=CH),
                                       b64[:, :, CH - 1:CH].broadcast_to([P, NCH, CH]), b64, ALU.subtract))
            link(dve.tensor_tensor(kIl, bc[:, :, SB // 2 - 1:SB // 2].broadcast_to([P, HP, NM]), bc[:, :, 0:NM], ALU.subtract))
            link(dve.tensor_tensor(kD[:, :, 0:NM], bc[:, :, NM - 1:NM].broadcast_to([P, HP, NM]), bc[:, :, 0:NM], ALU.subtract))
            link(dve.tensor_scalar(kIl, kIl, CLAMP, None, ALU.min))
            kIf = kI.rearrange("p a b n -> p (a b n)")
            dve.tensor_scalar(kIf, kIf, CLAMP, None, ALU.min).then_inc(sem("shifted"), 1)
            take(4)
            qk = proj[:, 0:2, :], proj[:, 2:4, :]
            dve.wait_ge(sem("decays"), 7)
            dve.wait_ge(sem("proj_dve"), 5)
            low, up = slice(0, DK), slice(DK, 2 * DK)
            for mine, other, dst in ((up, low, qE[1]), (low, up, qE[0])):
                link(dve.scalar_tensor_tensor(out=dst[mine], in0=qk[0][mine], scalar=DK ** -0.5, in1=qE[0][mine], op0=ALU.mult, op1=ALU.mult),
                     dve.tensor_scalar(qS[0 if mine is low else 1][mine], qk[0][mine, :, TP:NT], DK ** -0.5, None, ALU.mult))
                dve.memset(dst[other], 0.0).then_inc(sem("qk_ready"), 1)
                dve.memset(qS[0 if mine is low else 1][other], 0.0).then_inc(sem("qk_ready"), 1)
            dve.scalar_tensor_tensor(out=qI[:, :, 0:TP], in0=qk[0][:, :, 0:TP], scalar=DK ** -0.5, in1=qI[:, :, 0:TP],
                                     op0=ALU.mult, op1=ALU.mult).then_inc(sem("qk_ready"), 1)
            dve.tensor_tensor(kD, kD, qk[1][:, :, 0:TP], ALU.mult).then_inc(sem("qk_ready"), 1)
            dve.tensor_tensor(kIl, kIl, qk[1][:, :, 0:NM], ALU.mult).then_inc(sem("qk_ready"), 1)
            for a in range(HP):
                dve.tensor_tensor(kI[:, a], kI[:, a], qk[1][:, a, NM:TP].unsqueeze(1).broadcast_to([P, NSB, SEQ]),
                                  ALU.mult).then_inc(sem("qk_ready"), 1)
            dve.wait_ge(sem("proj_act"), 4)
            xa = proj[:, 8:12, :]
            w = lambda j, m: pv[:, CONV_W + 4 * j + m:CONV_W + 4 * j + m + 1]
            link(dve.tensor_copy(xp[:, :, 3:3 + TP], xa[:, :, 0:TP]))
            csv = cs[:, :, 0:24].rearrange("p m (b j) -> p m j b", j=3)
            for j in range(4):
                for m in range(MA):
                    src = xp[:, m, j:j + TP]
                    past = csv[:, m, j, :] if j < 3 else xa[:, m, TP:NT]
                    if j == 0:
                        cb = pv[:, CONV_B + m:CONV_B + m + 1]
                        link(dve.tensor_scalar(xc[:, m, 0:TP], src, w(j, m), cb, ALU.mult, ALU.add),
                             dve.tensor_scalar(xc[:, m, TP:NT], past, w(j, m), cb, ALU.mult, ALU.add))
                    else:
                        one = dve.scalar_tensor_tensor(out=xc[:, m, 0:TP], in0=src, scalar=w(j, m), in1=xc[:, m, 0:TP], op0=ALU.mult, op1=ALU.add)
                        two = dve.scalar_tensor_tensor(out=xc[:, m, TP:NT], in0=past, scalar=w(j, m), in1=xc[:, m, TP:NT], op0=ALU.mult, op1=ALU.add)
                        if j < 3:
                            link(one, two)
                        else:
                            one.then_inc(sem("xc_ready"), 1)
                            two.then_inc(sem("xc_ready"), 1)
            dve.wait_ge(sem("cm_ready"), 1)
            for c, (t0, n) in enumerate(chunks):
                dve.wait_ge(sem("scored"), c + 1)
                for half in range(2):
                    dve.tensor_tensor(PT[0:n, c, half:HB:2, 0:n],
                                      ps[0:n, 4 + 2 * (c % 2) + half, 0:128].rearrange("p (a t) -> p a t", a=HP)[:, :, 0:n],
                                      cm[0:n, 0:n].unsqueeze(1).broadcast_to([n, HP, n]), ALU.mult).then_inc(sem("masked"), 1)
            dve.wait_ge(sem("s0_in"), 16 * NB)
            link(dve.tensor_tensor(S0, S0, eS.rearrange("p a b -> p b a").unsqueeze(3).broadcast_to([P, NB, HP, DV]), ALU.mult))
            dve.wait_ge(sem("v_spread"), 1)
            dve.tensor_tensor(Sn, ps[:, 4:8, :].rearrange("p q (b a v) -> p (q b) a v", b=2, a=HP),
                              proj[:, 2:4, TP:NT].rearrange("p a b -> p b a").unsqueeze(3).broadcast_to([P, NB, HP, DV]), ALU.mult).then_inc(sem("v_used"), 1)
            dve.wait_ge(sem("v_used"), 1)
            dve.tensor_tensor(Sn, Sn, S0, ALU.add).then_inc(sem("sample_state"), 1)
            dve.wait_ge(sem("rg_sig"), 2 * MA)
            for m in range(MA):
                link(dve.tensor_scalar(rr[:, m, :], rr[:, m, :], nsp8[:, m:m + 1], None, ALU.mult))
            dve.engine_nop().then_inc(sem("log_a"), 1)
            link(dve.tensor_tensor(ii, ii, xc, ALU.mult))
            dve.wait_ge(sem("a_ready"), 2)
            link(dve.tensor_tensor(ii, ii, T2, ALU.mult))
            dve.wait_ge(sem("om_root"), 1)
            link(dve.tensor_tensor(ii, ii, tt, ALU.mult))
            link(dve.tensor_tensor(T2[:, :, 0:NB], aa[:, :, TP:NT], cs[:, :, 24:32], ALU.mult))
            link(dve.tensor_tensor(rr[:, :, TP:NT], T2[:, :, 0:NB], ii[:, :, TP:NT], ALU.add),
                 *[dve.tensor_tensor_scan(out=rr[:, m, 0:TP], data0=aa[:, m, 0:TP], data1=ii[:, m, 0:TP], initial=0.0,
                                          op0=ALU.mult, op1=ALU.add) for m in range(MA)])
            dve.engine_nop().then_inc(sem("b_used"), 1)
            link(dve.tensor_copy(OT[:, :, 0:3], xa[:, :, TP - 3:TP]), dve.tensor_copy(OT[:, :, 3:3 + NB], xa[:, :, TP:NT]),
                 dve.tensor_copy(OT[:, :, 3 + NB:NO], rr[:, :, TP - 1:NT]))
            dve.engine_nop().then_inc(sem("ot_ready"), 1)
            dve.wait_ge(sem("proj_act"), 12)
            link(dve.tensor_tensor(xc, rr, proj[:, 12:16, :], ALU.mult))
            dve.tensor_tensor(T2, xc, xc, ALU.mult).then_inc(sem("a_sq"), 1)
            for c in range(NCH + 1):
                dve.wait_ge(sem("st_done"), c + 1)
                if c >= 2:
                    dve.wait_ge(sem("o_chunk"), c)
                new, old = Sg[c % 2], Sg[(c - 1) % 2]
                if c == 0:
                    link(dve.tensor_copy(new, ps[:, 4, 0:HP * DV].rearrange("p (a v) -> p a v", a=HP)))
                else:
                    link(*[dve.scalar_tensor_tensor(out=new[:, a, :], in0=old[:, a, :], scalar=eb[:, a, c:c + 1],
                                                    in1=ps[:, 4 + c % 2, a * DV:(a + 1) * DV], op0=ALU.mult, op1=ALU.add) for a in range(HP)])
                dve.engine_nop().then_inc(sem("gla_state"), 1)
                if c == 2:
                    dve.wait_ge(sem("rows_turned"), 1)
                    dve.tensor_copy(OS, ps[0:NO, 7, :]).then_inc(sem("rows_ready"), 1)
            dve.wait_ge(sem("proj_done"), len(TILES))
            dve.wait_ge(sem("rstd_a"), 1)
            for m in range(MA):
                dve.scalar_tensor_tensor(out=uT[:, m, :], in0=xc[:, m, :], scalar=pv[:, GNA + m:GNA + m + 1], in1=aa[:, 0, :],
                                         op0=ALU.mult, op1=ALU.mult).then_inc(sem("mix_ready"), 1)
            dve.wait_ge(sem("o_done"), 1)
            dve.wait_ge(sem("o_sq"), HP)
            dve.wait_ge(sem("proj_act"), 16)
            for a in range(HP):
                dve.scalar_tensor_tensor(out=proj[:, 16 + 2 * a:18 + 2 * a, TP:NT], in0=sampled[:, a], scalar=pv[:, GNB:GNB + 1],
                                         in1=proj[:, 16 + 2 * a:18 + 2 * a, TP:NT], op0=ALU.mult, op1=ALU.mult).then_inc(sem("o_sampled"), 1)
            dve.wait_ge(sem("o_sq"), HP + 1)
            link(dve.scalar_tensor_tensor(out=proj[:, 16:20, 0:TP], in0=ps[:, 0:4, 0:TP], scalar=pv[:, GNB:GNB + 1], in1=proj[:, 16:20, 0:TP],
                                          op0=ALU.mult, op1=ALU.mult))
            dve.engine_nop().then_inc(sem("o_used"), 1)
            dve.wait_ge(sem("o_sampled"), HP)
            dve.wait_ge(sem("rstd_b"), 1)
            dve.tensor_tensor(uT[:, 4:8, :], proj[:, 16:20, :], T3, ALU.mult).then_inc(sem("mix_ready"), 1)
            for c in range(TC):
                r = rows_of[c]
                for n in range(2):
                    dve.wait_ge(sem("out_done"), 2 * c + n + 1)
                    dst = yacc[0:r, c, n * 512:(n + 1) * 512]
                    dve.tensor_tensor(dst, ps[0:r, 2 * c + n, :], dst, ALU.add).then_inc(sem("h_ready"), 1)
                dve.wait_ge(sem("ssq"), TC + c + 1)
                dve.tensor_scalar(ssq[:, c:c + 1], ssq[:, c:c + 1], 1.0 / D, EPS, ALU.mult, ALU.add).then_inc(sem("var"), 1)
                dve.wait_ge(sem("std"), c + 2)
                link(dve.reciprocal(rstd[:, c:c + 1], rstd[:, c:c + 1]))
                if c == 0:
                    dve.wait_ge(sem("router_in"), 48)
                dve.scalar_tensor_tensor(out=u2[:, c, :], in0=yacc[:, c, :], scalar=rstd[:, c:c + 1], in1=gff,
                                         op0=ALU.mult, op1=ALU.mult).then_inc(sem("u2_ready"), 1)
            dve.wait_ge(sem("slot_no_ready"), 1)
            dve.tensor_scalar(selz[:, :, 0:S], slot_no[:, 0:S].unsqueeze(1).broadcast_to([P, TC, S]), 0.0, None, ALU.mult).then_inc(sem("selz_edges"), 1)
            dve.tensor_scalar(selz[:, :, 2 * S:3 * S], slot_no[:, 0:S].unsqueeze(1).broadcast_to([P, TC, S]), 0.0, None, ALU.mult).then_inc(sem("selz_edges"), 1)
            for c in range(TC):
                dve.wait_ge(sem("uhi_ready"), c + 1)
                dve.tensor_tensor(ulo[:, c, :], u2[:, c, :], uhi[:, c, :].bitcast(fp32), ALU.subtract).then_inc(sem("ulo_ready"), 1)
            def low_halves(p, n, ahead=True, halves=(0, 1)):
                for q in halves:
                    if p not in NATIVE and (p, q) not in BY_POOL:
                        lower(dve, p, n, ahead, q)

            low_halves(*EARLY[0])
            dve.wait_ge(sem("lg_done"), 1)
            link(dve.tensor_copy(lg, ps[:, 6, 0:TC * NE].rearrange("p (c e) -> p c e", c=TC)))
            top = small[:, 66:66 + TC * 8].rearrange("p (c n) -> p c n", c=TC)
            link(*[dve.max(top[:, c, :], lg[:, c, :]) for c in range(TC)])
            v4 = top[:, :, TOPK - 1:TOPK].broadcast_to([P, TC, NE])
            link(dve.tensor_tensor(gtv, lg, v4, ALU.is_gt), dve.tensor_tensor(eq, lg, v4, ALU.is_equal))
            dve.tensor_tensor(em, lg, top[:, :, 0:1].broadcast_to([P, TC, NE]), ALU.subtract).then_inc(sem("lg_shift"), 1)
            link(dve.tensor_reduce(out=ssq, in_=gtv, axis=AX.X, op=ALU.add))
            link(dve.tensor_scalar(ssq, ssq, -1.0, float(TOPK), ALU.mult, ALU.add))
            link(*[dve.tensor_tensor_scan(out=mk[:, c, :], data0=ones[:, 0:NE], data1=eq[:, c, :], initial=0.0,
                                          op0=ALU.mult, op1=ALU.add) for c in range(TC)])
            link(dve.tensor_tensor(mk, mk, ssq.unsqueeze(2).broadcast_to([P, TC, NE]), ALU.is_le))
            link(dve.tensor_tensor(mk, mk, eq, ALU.mult))
            link(dve.tensor_tensor(mk, mk, gtv, ALU.add))
            dve.wait_ge(sem("tri_ready"), 2)
            dve.tensor_tensor(mk, mk, valid.unsqueeze(2).broadcast_to([P, TC, NE]), ALU.mult).then_inc(sem("mask_ready"), 1)
            dve.wait_ge(sem("mask_ready"), 1)
            dve.wait_ge(sem("lg_exp"), 1)
            link(dve.tensor_tensor(em, em, mk, ALU.mult))
            link(dve.tensor_reduce(out=ssq, in_=em, axis=AX.X, op=ALU.add))
            link(dve.tensor_scalar(ssq, ssq, 1e-30, None, ALU.max))
            link(dve.reciprocal(ssq, ssq))
            dve.tensor_tensor(em, em, ssq.unsqueeze(2).broadcast_to([P, TC, NE]), ALU.mult).then_inc(sem("gates_ready"), 1)
            dve.wait_ge(sem("gates_ready"), 1)
            low_halves(*EARLY[1])
            dve.wait_ge(sem("rank_done"), 1)
            link(dve.tensor_scalar(lg, ps[:, 7, 0:TC * NE].rearrange("p (c e) -> p c e", c=TC), 1.0, None, ALU.add))
            link(dve.tensor_tensor(lg, lg, mk, ALU.mult))
            rounds = NV // NE
            link(*[dve.tensor_scalar(pos[:, :, r * NE:(r + 1) * NE], lg, -1.0 - r * S, None, ALU.add) for r in range(rounds)],
                 dve.memset(pos[:, :, NV:NV + 2], -1.0),
                 dve.tensor_copy(gate[:, :, :], em),
                 dve.tensor_reduce(out=la0[:, 0:1], in_=ps[:, 7, TC * NE:(TC + 1) * NE], axis=AX.X, op=ALU.max))
            dve.engine_nop().then_inc(sem("pos_ready"), 1)
            dve.tensor_scalar(flag[:, :], la0[:, 0:1], float(S), None, ALU.is_gt).then_inc(sem("flag_ready"), 1)

            def one_hot(n):
                if not isinstance(n, int) or n >= 1:
                    dve.wait_ge(sem("gathered"), n)
                dve.tensor_tensor(selz[:, :, S:2 * S], slot_no[:, 0:S].unsqueeze(1).broadcast_to([P, TC, S]),
                                  pos[:, :, bass.ds(n, 1)].broadcast_to([P, TC, S]), ALU.is_equal).then_inc(sem("sel_ready"), 1)

            one_hot(0)
            one_hot(1)

            def body(i, ahead=True, between=True):
                do_i, do_j, do_m = lags(i, ahead, between)

                def lo(p, n, halves=(0, 1)):
                    if not early(p, n):
                        low_halves(p, n, ahead, halves)

                first = isinstance(i, int) and i == 0

                def add_biases(us):
                    for u in us:
                        c, n = divmod(u, 2)
                        dve.wait_ge(sem("bd_done"), u + 1)
                        dst = yacc[:, c, n * 512:(n + 1) * 512]
                        dve.tensor_tensor(dst, ps[:, 4 + n, :], dst, ALU.add).then_inc(sem("added"), 1)

                def collect(us):
                    for u in us:
                        c, n = divmod(u, 2)
                        dve.wait_ge(sem("scattered"), 6 * (i - 2) + u + 1)
                        if u == 0:
                            dve.wait_ge(sem("added"), 6 * (i - 2) + 6)
                        dst = yacc[:, c, n * 512:(n + 1) * 512]
                        dve.tensor_tensor(dst, ps[:, 6 + u % 2, :], dst, ALU.add).then_inc(sem("added"), 1)

                if do_i:
                    lo(0, i)
                    lo(1, i)
                if do_j:
                    dve.wait_ge(sem("gu_turned"), i)
                    for n in range(2):
                        dve.tensor_tensor(hS[:, n, :].rearrange("p (k s) -> p k s", k=8), ps[:, 6 + n, :].rearrange("p (k s) -> p k s", k=8),
                                          bguT[:, 8 * n:8 * n + 8, bass.ds(e_of(i - 1), 1)].broadcast_to([P, 8, S]), ALU.add).then_inc(sem("biased"), 1)
                    dve.wait_ge(sem("biased"), 2 * i)
                    dve.tensor_scalar(hS[:, 0, :], hS[:, 0, :], LIMIT, None, ALU.min).then_inc(sem("clipped"), 1)
                    dve.tensor_scalar(hS[:, 1, :], hS[:, 1, :], LIMIT, -LIMIT, ALU.min, ALU.max).then_inc(sem("lin_clipped"), 1)
                if do_m:
                    dve.wait_ge(sem("slot_gate_ready"), i - 1)
                    if not isinstance(i, int) or i >= 3:
                        dve.wait_ge(sem("scattered"), 6 * (i - 2))
                    dve.tensor_scalar(GT[:, :], ps[:, 6 if do_i else 0, 0:TC * P], 0.0, None, ALU.not_equal).then_inc(sem("gt_ready"), 1)
                if do_i:
                    lo(2, i)
                    lo(3, i, (0,))
                if do_m:
                    dve.wait_ge(sem("y_hi"), i - 1)
                    dve.scalar_tensor_tensor(out=ylo[:, :].rearrange("p (a n) -> p a n", a=2), in0=ps[:, 4:6, :], scalar=slot_gate,
                                             in1=yhi[:, :].bitcast(fp32).rearrange("p (a n) -> p a n", a=2),
                                             op0=ALU.mult, op1=ALU.subtract).then_inc(sem("y_lo"), 1)
                if do_j:
                    if do_m:
                        dve.wait_ge(sem("gt_turned"), i - 1)
                    dve.tensor_tensor(Gm[:, :, :], slot_no[:, :].unsqueeze(1).broadcast_to([P, TC, 2 * S]),
                                      pos[:, :, bass.ds(i - 1, 1)].broadcast_to([P, TC, 2 * S]), ALU.is_equal).then_inc(sem("gm_hot"), 1)
                    dve.wait_ge(sem("lin_clipped"), i)
                    dve.scalar_tensor_tensor(out=hS[:, 1, :], in0=hS[:, 1, :], scalar=1.0, in1=hS[:, 0, :], op0=ALU.add, op1=ALU.mult).then_inc(sem("product"), 1)
                if do_i:
                    lo(3, i, (1,))
                if do_m and (do_i or not do_j):
                    collect((0, 1))
                if first:
                    add_biases((0, 1))
                if do_j:
                    dve.wait_ge(sem("product"), i)
                    dve.wait_ge(sem("sig_ready"), i)
                    dve.tensor_tensor(hS[:, 1, :], hS[:, 1, :], hS[:, 0, :], ALU.mult).then_inc(sem("acted"), 1)
                    if not do_i:
                        lo(8, i - 1)
                if do_i:
                    lo(4, i)
                if do_m and (do_i or not do_j):
                    collect((2, 3))
                if first:
                    add_biases((2, 3))
                if do_i:
                    lo(5, i)
                if do_m and (do_i or not do_j):
                    collect((4, 5))
                if first:
                    add_biases((4, 5))
                if do_j:
                    dve.wait_ge(sem("act_hi"), i)
                    dve.tensor_tensor(actT[:, :, S:2 * S], hS[:, 1, :].rearrange("p (k s) -> p k s", k=KD),
                                      actT[:, :, 0:S].bitcast(fp32), ALU.subtract).then_inc(sem("act_lo"), 1)
                if do_i:
                    lo(6, i)
                    lo(7, i)
                if do_i and do_j:
                    lo(8, i - 1)
                if do_i:
                    one_hot(i + 2)
                if do_i and not do_j:
                    low_halves(*EARLY[2])
                if do_j:
                    lo(9, i - 1)
                    lo(10, i - 1)
                for n in range(2):
                    if do_i:
                        dve.wait_ge(sem("low_ready"), 2 * i + n + 1)
                        if n == 0 and (not isinstance(i, int) or i >= 1):
                            dve.wait_ge(sem("gu_turned"), i)
                        dve.tensor_tensor(guS[:, n * 1024:(n + 1) * 1024].rearrange("p (a n) -> p a n", a=2), ps[0:S, 2 * n:2 * n + 2, :],
                                          xr[0:S, :].rearrange("p (a n) -> p a n", a=2), ALU.add).then_inc(sem("guS_ready"), 1)
                    if do_j and n == 0:
                        lo(11, i - 1)
                    elif not do_j and do_i and n == 0:
                        low_halves(*EARLY[3])
                    if do_j and do_m and not do_i:
                        collect(((0, 1, 2, 3), (4, 5))[n])

            passes(dve, body)
            dve.wait_ge(sem("ssq"), 3 * TC)
            dve.tensor_scalar(ssq, ssq, 1.0 / D, EPS, ALU.mult, ALU.add).then_inc(sem("var"), 1)
            dve.wait_ge(sem("std"), 2 + TC)
            link(dve.reciprocal(rstd, rstd))
            dve.wait_ge(sem("gfin_in"), 16)
            for c in range(TC):
                dve.scalar_tensor_tensor(out=yout[:, c, :], in0=yacc[:, c, :], scalar=rstd[:, c:c + 1], in1=gfin,
                                         op0=ALU.mult, op1=ALU.mult).then_inc(sem("y_ready"), 1)

        @block.tensor
        def _(pe):
            pe.wait_ge(sem("ident_ready"), 1)
            pe.wait_ge(sem("par_in"), 16 * len(by_act))
            pe.wait_ge(sem("par_in_pool"), 16 * len(by_pool))
            pe.transpose(ps[:, 0, 0:47], pin[0:47, :], ident[0:47, 0:47])
            for m in range(MA):
                pe.transpose(ps[:, 1, 32 * m:32 * m + 32], cst[0:32, m * P:(m + 1) * P], ident[0:32, 0:32])
            for f in range(NF):
                last = pe.transpose(ps[:, 2, NE * f:NE * (f + 1)], bgr[0:NE, f * P:(f + 1) * P], ident[0:NE, 0:NE])
            last.then_inc(sem("par_turned"), 1)
            pe.wait_ge(sem("xn_ready"), TC)
            pe.wait_ge(sem("par_ready"), 3)
            for k in range(KD):
                for c in range(TC):
                    r = rows_of[c]
                    last = pe.transpose(ps[:, k, c * P:c * P + r], xn[0:r, c, k * P:(k + 1) * P], ident[0:r, 0:r])
                last.then_inc(sem("u_turned"), 1)
            pe.wait_ge(sem("uT_ready"), KD)

            def project(t):
                name, w, _ = TILES[t]
                rows = GR if t == 0 else P
                pe.wait_ge(sem(name), 16)
                if t >= 4:
                    who, n = evacuator(t - 4)
                    pe.wait_ge(sem(who), n)
                for k in range(KD):
                    last = pe.matmul(ps[0:rows, t % 4, 0:NT], w(k), uT[:, k, :], start=(k == 0), stop=(k == KD - 1))
                last.then_inc(sem("proj_done"), 1)

            project(0)
            project(1)
            pe.wait_ge(sem("proj_dve"), 1)
            pe.wait_ge(sem("gup_in"), 16)
            for a in range(HP):
                pe.matmul(ps[:, 4 + a, 0:NT], gup[:, a * P:(a + 1) * P], lrT[:, :], start=True, stop=True).then_inc(sem("z_done"), 1)
            for t in (2, 3, 4, *XA_TILES, *V_TILES):
                project(t)
            pe.wait_ge(sem("proj_act"), 8)
            pe.wait_ge(sem("qk_ready"), 6)
            for c, (t0, n) in enumerate(chunks):
                if c >= 2:
                    pe.wait_ge(sem("vt"), 2 * (c - 1))
                for h in range(HB):
                    pe.transpose(ps[0:n, 4 + 2 * (c % 2), h * DV:(h + 1) * DV], proj[:, 4 + h, t0:t0 + n], ident[:, :])
                for a in range(HP):
                    last = pe.transpose(ps[0:n, 5 + 2 * (c % 2), a * P:(a + 1) * P], kD[:, a, t0:t0 + n], ident[:, :])
                last.then_inc(sem("turned"), 1)
            pe.wait_ge(sem("vt"), 2 * NCH)
            for h in range(HB):
                last = pe.transpose(ps[0:NB, 6, h * DV:(h + 1) * DV], proj[:, 4 + h, TP:NT], ident[:, :])
            last.then_inc(sem("vs_turned"), 1)
            pe.wait_ge(sem("qk_ready"), 9)
            pe.wait_ge(sem("vt"), 2 * (NCH + 1))
            pe.wait_ge(sem("vs_ready"), 1)
            for c, (t0, n) in enumerate(chunks):
                if c >= 2:
                    pe.wait_ge(sem("masked"), 2 * (c - 1))
                for h in range(HB):
                    a, r = h // 2, slice(64 * (h % 2), 64 * (h % 2) + 64)
                    for i in range(max(1, n // SB)):
                        keys = kIl[r, a, :] if c == 0 else kI[r, a, i, (c - 1) * CH:c * CH]
                        col = a * CH + SB * i
                        last = pe.matmul(ps[0:n, 4 + 2 * (c % 2) + h % 2, col:col + SB], keys,
                                         qI[r, a, t0 + SB * i:t0 + SB * (i + 1)], start=True, stop=True)
                last.then_inc(sem("scored"), 1)
            pe.wait_ge(sem("masked"), 2 * (NCH + 1))
            vh = vs[0:NB, :].rearrange("p (a h v) -> p a h v", a=HP, h=2)
            for b in range(NB):
                for half in range(2):
                    last = pe.matmul(ps[64 * half:64 * half + 64, 4 + b // 2, (b % 2) * 256:(b % 2) * 256 + 256],
                                     ident[0:NB, b:b + 1].broadcast_to([NB, 64]), vh[:, :, half, :], start=True, stop=True)
            last.then_inc(sem("v_spread"), 1)
            for t in YA_TILES:
                project(t)
            pe.wait_ge(sem("wrg_in"), 16 * 4 * MA)
            pe.wait_ge(sem("xc_ready"), 2 * MA)
            pe.wait_ge(sem("v_used"), 1)
            for m in range(MA):
                for g, wt in enumerate((WA, WX)):
                    if m >= 2:
                        pe.wait_ge(sem("rg_sig"), 2 * (m - 2) + g + 1)
                    pe.matmul(ps[:, 4 + 2 * (m % 2) + g, 0:NT], wt[:, m, :], xc[:, m, :], start=True, stop=True).then_inc(sem("rg_done"), 1)
            for t in G_TILES:
                project(t)
            pe.wait_ge(sem("proj_act"), 16)
            pe.wait_ge(sem("rg_sig"), 2 * MA)
            pe.wait_ge(sem("masked"), 2 * (NCH + 1))
            for c, (t0, n) in enumerate(chunks):
                if c >= 2:
                    pe.wait_ge(sem("gla_state"), c - 1)
                for h in range(HB):
                    a, o = h // 2, 64 * (h % 2)
                    last = pe.matmul(ps[o:o + 64, 4 + c % 2, a * DV:(a + 1) * DV], KT[0:n, c, h * DK:(h + 1) * DK],
                                     VT[0:n, c, h * DV:(h + 1) * DV], start=True, stop=True)
                last.then_inc(sem("st_done"), 1)
                for h in range(HB):
                    a, o = h // 2, 64 * (h % 2)
                    last = pe.matmul(ps[:, h, t0:t0 + n], VT[0:n, c, h * DV:(h + 1) * DV], PT[0:n, c, h, 0:n], start=True, stop=(c == 0))
                    if c >= 1:
                        if h == 0:
                            pe.wait_ge(sem("gla_state"), c)
                        last = pe.matmul(ps[:, h, t0:t0 + n], Sg[(c - 1) % 2][:, a, :], qE[h % 2][:, a, t0:t0 + n], start=False, stop=True)
                last.then_inc(sem("o_chunk"), 1)
                if c == 1:
                    pe.wait_ge(sem("ot_ready"), 1)
                    for m in range(MA):
                        last = pe.transpose(ps[0:NO, 7, m * P:(m + 1) * P], OT[:, m, :], ident[:, :])
                    last.then_inc(sem("rows_turned"), 1)
                    pe.wait_ge(sem("rg_sig"), 2 * MA)
                    pe.wait_ge(sem("a_sq"), 1)
                    for m in range(MA):
                        last = pe.matmul(ps[:, 6, 0:NT], ones[:, :], T2[:, m, :], start=(m == 0), stop=(m == MA - 1))
                    last.then_inc(sem("a_sum"), 1)
            pe.wait_ge(sem("gla_state"), NCH + 1)
            pe.wait_ge(sem("sample_state"), 1)
            pe.wait_ge(sem("rows_ready"), 1)
            for a in range(HP):
                for b in range(NB):
                    pair = small[:, qS_AT[0] + a * NB + b:qS_AT[1] + a * NB + b + 1:qS_AT[1] - qS_AT[0]]
                    last = pe.matmul(ps[:, 7, (a * NB + b) * 2:(a * NB + b) * 2 + 2], Sn[:, b, a, :], pair, start=True, stop=True)
            last.then_inc(sem("o_done"), 1)
            pe.wait_ge(sem("o_sq"), HP + 1)
            pe.wait_ge(sem("o_sampled"), HP)
            pe.wait_ge(sem("rows_ready"), 1)
            pe.wait_ge(sem("rstd_a"), 1)
            for h in range(HB):
                last = pe.matmul(ps[:, 4 + h, 0:NT], ones[:, :], tt[:, h, :], start=True, stop=True)
            last.then_inc(sem("b_sum"), 1)
            pe.wait_ge(sem("wout_in"), 16)

            def project_out(c, ks=range(KD)):
                r = rows_of[c]
                for n in range(2):
                    for k in ks:
                        last = pe.matmul(ps[0:r, 2 * c + n, :], uT[:, k, c * P:c * P + r], wout[:, k, n * 512:(n + 1) * 512], start=(k == 0), stop=(k == KD - 1))
                    if k == KD - 1:
                        last.then_inc(sem("out_done"), 1)

            def turn_u2(c):
                pe.wait_ge(sem("u2_ready"), c + 1)
                for q in range(2):
                    for k in range(4):
                        last = pe.transpose(ps[:, 2 * c + q, k * P:(k + 1) * P], u2[:, c, (4 * q + k) * P:(4 * q + k + 1) * P], ident[:, :])
                    last.then_inc(sem("u2_turned"), 1)

            def logits(c):
                pe.wait_ge(sem("u2T_ready"), 2 * c + 2)
                for k in range(KD):
                    pe.matmul(ps[:, 6, c * NE:(c + 1) * NE], u2T[:, k, c * P:(c + 1) * P], wr[:, k, :], start=(k == 0), stop=False)
                return pe.matmul(ps[:, 6, c * NE:(c + 1) * NE], ones[0:1, :], brow[0:1, :], start=False, stop=True)

            pe.wait_ge(sem("mix_ready"), MA)
            pe.wait_ge(sem("o_used"), 1)
            project_out(0, range(MA))
            pe.wait_ge(sem("mix_ready"), MA + 1)
            project_out(0, range(MA, KD))
            project_out(1)
            turn_u2(0)
            project_out(2)
            turn_u2(1)
            logits(0)
            logits(1)
            turn_u2(2)
            logits(2).then_inc(sem("lg_done"), 1)
            pe.wait_ge(sem("mask_ready"), 1)
            for c in range(TC):
                pe.matmul(ps[:, 7, c * NE:(c + 1) * NE], tri, mk[:, c, :], start=True, stop=(c == 0))
                for b in range(c):
                    pe.matmul(ps[:, 7, c * NE:(c + 1) * NE], ones[:, :], mk[:, b, :], start=False, stop=(b == c - 1))
            for c in range(TC):
                last = pe.matmul(ps[:, 7, TC * NE:(TC + 1) * NE], ones[:, :], mk[:, c, :], start=(c == 0), stop=(c == TC - 1))
            last.then_inc(sem("rank_done"), 1)
            pe.wait_ge(sem("gates_ready"), 1)
            for c in range(TC):
                last = pe.transpose(ps[0:NE, 0, c * P:(c + 1) * P], em[:, c, :], ident[:, :])
            last.then_inc(sem("gd_turned"), 1)
            pe.wait_ge(sem("gd_ready"), 1)
            pe.wait_ge(sem("ulo_ready"), TC)
            pe.wait_ge(sem("selz_edges"), 2)

            def gather(n):
                pe.wait_ge(sem("sel_ready"), n + 1)
                for w in range(2):
                    cols = slice(w * 512, (w + 1) * 512)
                    for c in range(TC):
                        pe.matmul(ps[:, 6 + w, :], selz[:, c, S:3 * S], uhi[:, c, cols], start=(c == 0), stop=False)
                        last = pe.matmul(ps[:, 6 + w, :], selz[:, c, 0:2 * S], ulo[:, c, cols], start=False, stop=(c == TC - 1))
                last.then_inc(sem("gathered"), 1)

            def turn_rows(n):
                pe.wait_ge(sem("xr_ready"), n + 1)
                for k in range(KD):
                    last = pe.transpose(ps[:, 6 + k // 4, (k % 4) * P:(k % 4 + 1) * P], xr[:, k * P:(k + 1) * P], ident[:, :])
                last.then_inc(sem("x_turned"), 1)

            pe.wait_ge(sem("pos_ready"), 1)
            gather(0)
            turn_rows(0)

            def body(i, ahead=True, between=True):
                do_i, do_j, do_m = lags(i, ahead, between)

                def products(p, n, pairs):
                    for q in range(2):
                        if p in NATIVE:
                            if q == 0:
                                pe.wait_ge(sem(f"piece_in{p}"), 16 * n + 16)
                        else:
                            who, at = low_order(p, n, ahead, q)
                            pe.wait_ge(sem(who), at)
                        for dst, x2, col, first, final in pairs[q]:
                            cols = slice(col, col + 512)
                            if p in NATIVE:
                                last = pe.matmul(dst, x2.bitcast(fp32), raw[:, p, q * 1024 + col:q * 1024 + col + 512], start=first, stop=final)
                            else:
                                pe.matmul(dst, x2, ringhi[:, ring_slot[p, q], cols], start=first, stop=False)
                                last = pe.matmul(dst, x2, ringlo[:, ring_slot[p, q], cols], start=False, stop=final)
                        if p not in NATIVE:
                            last.then_inc(sem("split_used"), 1)
                        elif q == 1:
                            last.then_inc(sem(f"native_used{p}"), 1)

                def gu(p):
                    products(p, i, [[(ps[:, n, :], xT[:, p, :], (n % 2) * 512, p == 0, p == 7) for n in (2 * q, 2 * q + 1)] for q in range(2)])

                def dn(p):
                    products(p, i - 1, [[(ps[:, 4 + n, :], actT[:, 2 * (p - 8) + q, :], n * 512, p == 8 and q == 0, p == 11 and q == 1)
                                         for n in range(2)] for q in range(2)])

                first = isinstance(i, int) and i == 0

                def biases(us):
                    for u in us:
                        c, n = divmod(u, 2)
                        if u == 0:
                            pe.wait_ge(sem("bdn_in"), 16)
                        if u >= 2:
                            pe.wait_ge(sem("added"), u - 1)
                        pe.matmul(ps[:, 4 + n, :], GTd[:, c * P:(c + 1) * P], bdn[:, n * 512:(n + 1) * 512], start=True, stop=True).then_inc(sem("bd_done"), 1)

                def scatter(us):
                    for u in us:
                        c, n = divmod(u, 2)
                        if u >= 2:
                            pe.wait_ge(sem("added"), 6 * (i - 1) + u - 1)
                        else:
                            pe.wait_ge(sem("gt_ready"), i - 1)
                            pe.wait_ge(sem("y_lo"), i - 1)
                            if do_j and not do_i:
                                pe.wait_ge(sem("biased"), 2 * i)
                            elif not do_j:
                                pe.wait_ge(sem("added"), 6 * (i - 1))
                        pe.matmul(ps[:, 6 + n, :], GT[:, c * P:(c + 1) * P], yhi[:, n * 512:(n + 1) * 512], start=True, stop=False)
                        pe.matmul(ps[:, 6 + n, :], GT[:, c * P:(c + 1) * P], ylo[:, n * 512:(n + 1) * 512], start=False, stop=True).then_inc(sem("scattered"), 1)

                def turn_gates():
                    pe.wait_ge(sem("gm_ready"), i - 1)
                    pe.wait_ge(sem("biased"), 2 * (i if do_i else i - 1))
                    for c in range(TC):
                        last = pe.transpose(ps[:, 6 if do_i else 0, c * P:(c + 1) * P], Gm[:, c, :], ident[:, :])
                    last.then_inc(sem("gt_turned"), 1)

                if do_i:
                    pe.wait_ge(sem("xT_ready"), i + 1)
                    if do_j:
                        pe.wait_ge(sem("guS_ready"), 2 * i)
                    gu(0)
                elif do_j:
                    pe.wait_ge(sem("guS_ready"), 2 * i)
                    turn_gates()
                if do_j:
                    for f in range(NF):
                        last = pe.transpose(ps[:, 6 + f // 8, (f % 8) * S:(f % 8 + 1) * S], guS[:, f * P:(f + 1) * P], ident[0:S, 0:S])
                    last.then_inc(sem("gu_turned"), 1)
                if do_i:
                    gu(1)
                if do_m and (do_i or not do_j):
                    turn_gates()
                if do_i:
                    gu(2)
                if do_m and (do_i or not do_j):
                    scatter((0, 1))
                elif first:
                    biases((0, 1))
                if do_i:
                    gu(3)
                if do_m and (do_i or not do_j):
                    scatter((2, 3))
                elif first:
                    biases((2, 3))
                if do_i:
                    gu(4)
                if do_m and (do_i or not do_j):
                    scatter((4, 5))
                elif first:
                    biases((4, 5))
                if do_i:
                    gu(5)
                    gu(6)
                    if do_m:
                        pe.wait_ge(sem("added"), 6 * i)
                    elif do_j:
                        pe.wait_ge(sem("biased"), 2 * i)
                    gather(i + 1)
                    gu(7)
                elif do_j:
                    scatter((0, 1))
                if do_j:
                    pe.wait_ge(sem("act_lo"), i)
                    if do_m:
                        pe.wait_ge(sem("y_lo"), i - 1)
                    dn(8)
                if do_i:
                    turn_rows(i + 1)
                if do_j:
                    for p, us in ((9, (2, 3)), (10, (4, 5)), (11, ())):
                        if do_m and not do_i:
                            scatter(us)
                        dn(p)

            passes(pe, body)


_INS = ["x_prompt", "x_sample", "state_conv", "state_lru", "state_gla", "meta", "g_mix", "w_in", "conv_w", "conv_b",
        "w_rg_a", "b_rg_a", "w_rg_x", "b_rg_x", "lam", "gn_a", "w_gate_up", "b_gate", "gn_b", "w_out", "g_ffn",
        "w_router", "b_router", "w_gu", "b_gu", "w_down", "b_down", "g_final"]
_OUTS = [("y_p", (1, 256, 1024)), ("y_s", (8, 1, 1024)), ("conv_p", (1, 1, 3, 512)), ("lru_p", (1, 1, 512)),
         ("gla_p", (1, 1, 4, 64, 128)), ("conv_s", (1, 8, 3, 512)), ("lru_s", (1, 8, 512)), ("gla_s", (1, 8, 4, 64, 128))]


def kernel(**inputs):
    import numpy as np
    import concourse.bacc as bacc
    from concourse.bass_utils import run_bass_kernel_spmd

    nc = bacc.Bacc("TRN2", target_bir_lowering=False, num_devices=1)
    arrays, ins, outs = {}, {}, {}
    for name in _INS:
        a = np.ascontiguousarray(inputs[name])
        arrays[f"in_{name}"] = a
        ins[name] = nc.dram_tensor(f"in_{name}", a.shape, mybir.dt.from_np(a.dtype), kind="ExternalInput").ap()
    for name, shape in _OUTS:
        outs[name] = nc.dram_tensor(f"out_{name}", shape, mybir.dt.float32, kind="ExternalOutput").ap()
    hybrid_layer_kernel(nc, ins, outs)
    r = run_bass_kernel_spmd(nc, [arrays], core_ids=[0])
    return tuple(r.results[0][f"out_{name}"] for name, _ in _OUTS)
```
